# Optimizing a Trainium2 kernel written in Bass

```python
import functools
import jax, jax.numpy as jnp
from jax import lax
import numpy as np

D_MODEL = 1024
BATCH = 1
SEQ = 1024
DEPTH = 1
DEC_BATCH = 8
DEC_SEQ = 8
PAST_LEN = 1024
PAGE_SIZE = 128

N_HEADS = 8
QK_NOPE = 64
QK_ROPE = 32
V_HEAD = 64
Q_RANK = 384
KV_RANK = 256
MLA_WIDTH = N_HEADS * V_HEAD
QK_SCALE = (QK_NOPE + QK_ROPE) ** -0.5
ROPE_BASE = 10000.0
Q_BLOCK = 128
N_GROUPS = 8
GROUP_DIM = 64
GMLP_WIDTH = N_GROUPS * GROUP_DIM
CHUNK = 128
OFF_KV = Q_RANK
OFF_KR = OFF_KV + KV_RANK
OFF_G = OFF_KR + QK_ROPE
IN_COLS = OFF_G + 2 * GMLP_WIDTH
MIX_WIDTH = MLA_WIDTH + GMLP_WIDTH
D_FF = -(-8 * D_MODEL // (3 * 256)) * 256
EPS = 1e-6

kernel_name = "hymba_mla_gmlp_decoder_step"

def rmsnorm(x, g):
    xf = x.astype(jnp.float32)
    y = xf * lax.rsqrt(jnp.mean(xf * xf, axis=-1, keepdims=True) + EPS)
    return (y * g.astype(jnp.float32)).astype(x.dtype)

def layernorm(x, g, b):
    xf = x.astype(jnp.float32)
    mu = jnp.mean(xf, axis=-1, keepdims=True)
    xc = xf - mu
    y = xc * lax.rsqrt(jnp.mean(xc * xc, axis=-1, keepdims=True) + EPS)
    return (y * g.astype(jnp.float32) + b.astype(jnp.float32)).astype(x.dtype)

def rope(x, pos):
    half = QK_ROPE // 2
    inv = ROPE_BASE ** (-jnp.arange(half, dtype=jnp.float32) / half)
    ang = pos.astype(jnp.float32)[:, None] * inv[None, :]
    bshape = (ang.shape[0],) + (1,) * (x.ndim - 3) + (half,)
    c = jnp.cos(ang).reshape(bshape)
    s = jnp.sin(ang).reshape(bshape)
    xf = x.astype(jnp.float32)
    x1, x2 = xf[..., :half], xf[..., half:]
    return jnp.concatenate([x1 * c - x2 * s, x1 * s + x2 * c], axis=-1).astype(x.dtype)

def mixer_front(h, pos, w_in, q_norm_g, w_q_up, kv_norm_g, w_uk, v_norm_g, v_norm_b):
    B, S, _ = h.shape
    z = h @ w_in
    c_q = z[..., :OFF_KV]
    c_kv = rmsnorm(z[..., OFF_KV:OFF_KR], kv_norm_g)
    k_r = rope(z[..., OFF_KR:OFF_G], pos)
    q = (rmsnorm(c_q, q_norm_g) @ w_q_up).reshape(B, S, N_HEADS, QK_NOPE + QK_ROPE)
    q_lat = jnp.einsum('bshn,rhn->bshr', q[..., :QK_NOPE], w_uk) * QK_SCALE
    q_rope = rope(q[..., QK_NOPE:], pos) * QK_SCALE
    zg = jax.nn.gelu(z[..., OFF_G:], approximate=False)
    u = zg[..., :GMLP_WIDTH]
    v = layernorm(zg[..., GMLP_WIDTH:], v_norm_g, v_norm_b)
    return q_lat, q_rope, c_kv, k_r, u, v

def mla_prompt_attend(q_lat, q_rope, c_kv, k_r):
    B, S = q_lat.shape[:2]
    nb = S // Q_BLOCK
    ql = q_lat.reshape(B, nb, Q_BLOCK, N_HEADS, KV_RANK).transpose(1, 0, 2, 3, 4)
    qr = q_rope.reshape(B, nb, Q_BLOCK, N_HEADS, QK_ROPE).transpose(1, 0, 2, 3, 4)
    kpos = jnp.arange(S)

    def block(args):
        i, qlb, qrb = args
        s = (jnp.einsum('bqhr,bkr->bhqk', qlb, c_kv)
             + jnp.einsum('bqhp,bkp->bhqk', qrb, k_r)).astype(jnp.float32)
        qpos = i * Q_BLOCK + jnp.arange(Q_BLOCK)
        s = jnp.where(kpos[None, :] <= qpos[:, None], s, -jnp.inf)
        p = jax.nn.softmax(s, axis=-1).astype(c_kv.dtype)
        return jnp.einsum('bhqk,bkr->bqhr', p, c_kv)

    o = lax.map(block, (jnp.arange(nb), ql, qr))
    return o.transpose(1, 0, 2, 3, 4).reshape(B, S, N_HEADS, KV_RANK)

def mla_sample_attend(q_lat, q_rope, c_kv, k_r, cache_ckv, cache_krope, page_table, layer):
    DB, T = q_lat.shape[:2]
    past_c = cache_ckv[layer, page_table].reshape(DB, -1, KV_RANK)
    past_r = cache_krope[layer, page_table].reshape(DB, -1, QK_ROPE)
    P = past_c.shape[1]
    s_past = (jnp.einsum('bqhr,bkr->bhqk', q_lat, past_c)
              + jnp.einsum('bqhp,bkp->bhqk', q_rope, past_r)).astype(jnp.float32)
    s_new = (jnp.einsum('bqhr,bkr->bhqk', q_lat, c_kv)
             + jnp.einsum('bqhp,bkp->bhqk', q_rope, k_r)).astype(jnp.float32)
    causal = jnp.tril(jnp.ones((T, T), dtype=bool))
    s_new = jnp.where(causal, s_new, -jnp.inf)
    p = jax.nn.softmax(jnp.concatenate([s_past, s_new], axis=-1), axis=-1).astype(c_kv.dtype)
    return (jnp.einsum('bhqk,bkr->bqhr', p[..., :P], past_c)
            + jnp.einsum('bhqk,bkr->bqhr', p[..., P:], c_kv))

def spatial_gate(u, v, w_s, b_s):
    B, S, _ = v.shape
    L = min(S, CHUNK)
    nc = S // L
    w = jnp.where(jnp.tril(jnp.ones((L, L), dtype=bool)), w_s[:, :L, :L], 0)
    vc = v.reshape(B, nc, L, N_GROUPS, GROUP_DIM)
    mix = jnp.einsum('gij,bcjgd->bcigd', w, vc) + b_s[:, :L].T[None, None, :, :, None]
    return u * mix.reshape(B, S, GMLP_WIDTH)

def trunk_layer(x, pos, attend, norm1_g, w_in, q_norm_g, w_q_up, kv_norm_g, w_uk, w_uv,
                v_norm_g, v_norm_b, w_spatial, b_spatial, out_norm_mla_g, out_norm_gmlp_g,
                w_out, norm2_g, w_gate, w_up, w_down):
    B, S, _ = x.shape
    h = rmsnorm(x, norm1_g)
    q_lat, q_rope, c_kv, k_r, u, v = mixer_front(h, pos, w_in, q_norm_g, w_q_up, kv_norm_g,
                                                 w_uk, v_norm_g, v_norm_b)
    o_lat = attend(q_lat, q_rope, c_kv, k_r)
    a = jnp.einsum('bshr,rhv->bshv', o_lat, w_uv).reshape(B, S, MLA_WIDTH)
    g = spatial_gate(u, v, w_spatial, b_spatial)
    merged = jnp.concatenate([rmsnorm(a, out_norm_mla_g), rmsnorm(g, out_norm_gmlp_g)], axis=-1)
    x = x + merged @ w_out
    h2 = rmsnorm(x, norm2_g)
    x = x + (jax.nn.silu(h2 @ w_gate) * (h2 @ w_up)) @ w_down
    return x, c_kv, k_r, v

def setup_inputs(seed: int = 0) -> dict:
    key = jax.random.key(seed)
    ks = iter(jax.random.split(key, 32))
    f32 = jnp.float32

    def nrm(shape, scale):
        return jax.random.normal(next(ks), shape, f32) * scale

    def gain(shape):
        return 1.0 + 0.05 * jax.random.normal(next(ks), shape, f32)

    n_pages = PAST_LEN // PAGE_SIZE
    n_used = DEC_BATCH * n_pages
    n_pool = n_used + (n_used + 3) // 4
    page_table = jax.random.permutation(next(ks), n_pool)[:n_used].reshape(DEC_BATCH, n_pages).astype(jnp.int32)

    return {
        "x_prompt": nrm((BATCH, SEQ, D_MODEL), 1.0),
        "x_sample": nrm((DEC_BATCH, DEC_SEQ, D_MODEL), 1.0),
        "cache_ckv": nrm((DEPTH, n_pool, PAGE_SIZE, KV_RANK), 1.0),
        "cache_krope": nrm((DEPTH, n_pool, PAGE_SIZE, QK_ROPE), 1.0),
        "page_table": page_table,
        "norm1_g": gain((DEPTH, D_MODEL)),
        "w_in": nrm((DEPTH, D_MODEL, IN_COLS), D_MODEL ** -0.5),
        "q_norm_g": gain((DEPTH, Q_RANK)),
        "w_q_up": nrm((DEPTH, Q_RANK, N_HEADS * (QK_NOPE + QK_ROPE)), Q_RANK ** -0.5),
        "kv_norm_g": gain((DEPTH, KV_RANK)),
        "w_uk": nrm((DEPTH, KV_RANK, N_HEADS, QK_NOPE), KV_RANK ** -0.5),
        "w_uv": nrm((DEPTH, KV_RANK, N_HEADS, V_HEAD), KV_RANK ** -0.5),
        "v_norm_g": gain((DEPTH, GMLP_WIDTH)),
        "v_norm_b": nrm((DEPTH, GMLP_WIDTH), 0.02),
        "w_spatial": nrm((DEPTH, N_GROUPS, CHUNK, CHUNK), CHUNK ** -0.5),
        "b_spatial": 1.0 + nrm((DEPTH, N_GROUPS, CHUNK), 0.1),
        "out_norm_mla_g": gain((DEPTH, MLA_WIDTH)),
        "out_norm_gmlp_g": gain((DEPTH, GMLP_WIDTH)),
        "w_out": nrm((DEPTH, MIX_WIDTH, D_MODEL), MIX_WIDTH ** -0.5),
        "norm2_g": gain((DEPTH, D_MODEL)),
        "w_gate": nrm((DEPTH, D_MODEL, D_FF), D_MODEL ** -0.5),
        "w_up": nrm((DEPTH, D_MODEL, D_FF), D_MODEL ** -0.5),
        "w_down": nrm((DEPTH, D_FF, D_MODEL), D_FF ** -0.5),
        "final_norm_g": gain((D_MODEL,)),
    }

def reference(x_prompt, x_sample, cache_ckv, cache_krope, page_table, norm1_g, w_in, q_norm_g,
              w_q_up, kv_norm_g, w_uk, w_uv, v_norm_g, v_norm_b, w_spatial, b_spatial,
              out_norm_mla_g, out_norm_gmlp_g, w_out, norm2_g, w_gate, w_up, w_down, final_norm_g):
    S = x_prompt.shape[1]
    T = x_sample.shape[1]
    pos_p = jnp.arange(S)
    pos_s = PAST_LEN + jnp.arange(T)
    xp, xs = x_prompt, x_sample
    ckv_p, kr_p, ckv_s, kr_s, v_s = [], [], [], [], []
    for l in range(DEPTH):
        lw = (norm1_g[l], w_in[l], q_norm_g[l], w_q_up[l], kv_norm_g[l], w_uk[l], w_uv[l],
              v_norm_g[l], v_norm_b[l], w_spatial[l], b_spatial[l], out_norm_mla_g[l],
              out_norm_gmlp_g[l], w_out[l], norm2_g[l], w_gate[l], w_up[l], w_down[l])
        xp, c1, r1, _ = trunk_layer(xp, pos_p, mla_prompt_attend, *lw)
        attend_s = functools.partial(mla_sample_attend, cache_ckv=cache_ckv, cache_krope=cache_krope,
                                     page_table=page_table, layer=l)
        xs, c2, r2, v2 = trunk_layer(xs, pos_s, attend_s, *lw)
        ckv_p.append(c1)
        kr_p.append(r1)
        ckv_s.append(c2)
        kr_s.append(r2)
        v_s.append(v2)
    y_prompt = rmsnorm(xp, final_norm_g)
    y_sample = rmsnorm(xs, final_norm_g)
    ckv_prompt = jnp.stack(ckv_p)
    krope_prompt = jnp.stack(kr_p)
    ckv_sample = jnp.stack(ckv_s)
    krope_sample = jnp.stack(kr_s)
    gmlp_v_sample = jnp.stack(v_s)
    return (y_prompt, y_sample, ckv_prompt, krope_prompt, ckv_sample, krope_sample, gmlp_v_sample)


_drawn_inputs = setup_inputs


def setup_inputs(seed=0):
    import zlib

    import numpy as np

    out = dict(_drawn_inputs(seed))
    spreads = {}
    factors = {'v_norm_b': 2.873}
    for name, (base, spread) in spreads.items():
        noise = np.random.default_rng([zlib.crc32(name.encode()), seed]).standard_normal(out[name].shape)
        drawn = base * np.exp(spread * noise) if base else spread * noise
        out[name] = __import__('jax').numpy.asarray(drawn.astype(out[name].dtype))
    for name, factor in factors.items():
        out[name] = (out[name] * factor).astype(out[name].dtype)
    return out
```

```python
from contextlib import ExitStack

import concourse.bass as bass
from concourse import mybir

F32 = mybir.dt.float32
F32R = mybir.dt.float32r
I32 = mybir.dt.int32
ALU = mybir.AluOpType
ACT = mybir.ActivationFunctionType
AX = mybir.AxisListType

P = 128
D = 1024
SEQ = 1024
NB, TS = 8, 8
NS = NB * TS
T = SEQ + NS
KD = D // P
H = 8
NOPE, ROPE, VH = 64, 32, 64
QK = NOPE + ROPE
QR, KVR = 384, 256
KQ, KC = QR // P, KVR // P
G, GD = 8, 64
GW = G * GD
KG = GW // P
FF = 2816
NF = FF // P
PAGES, PAGE, POOL = 8, 128, 80
EPS = 1e-6
SCALE = QK ** -0.5
CH = [(0, 384), (384, 384), (768, 320)]
NC = len(CH)
NT = 9
PAIRS = H // 2
UNITS = 4 * PAIRS
REC = 2 * KVR
CB = 3
NEW = PAGES * PAGE
GEN = 2 * NC + 2

N_V, N_SP, N_U, N_IN = 0, 4, 5, 9
N_HEAD = N_IN + KQ + KC + 1
N_OUT = N_HEAD + 2 * PAIRS
N_FF = N_OUT + KD
BODY = 6


def rows(t):
    return P if t < NT - 1 else NS


def tr_count(u):
    return 12 * (u // 2) + 4 * (u % 2)


def gens_at(u, kt):
    return range(2 * kt, 2 * kt + 2) if u % 4 == 3 and u + 1 < UNITS and kt < 4 else ()


def row_at(u, kt):
    qi = kt - (4 if u % 4 == 3 else 0)
    return qi if u + 1 < UNITS and 0 <= qi < 4 else None


def prob_at(qt):
    return P * (qt * (qt + 1) // 2)


def build(nc, d):
    ctx = ExitStack()
    with ctx:
        class Region:
            def __init__(self, start, end=None):
                self.start, self.here, self.end = start, start, end

            def put(self, name, shape, dt=F32):
                n = 4
                for s in shape[1:]:
                    n *= s
                t = nc.alloc_sbuf_tensor_at(name, shape, dt, offset=self.here)
                self.here += (n + 31) // 32 * 32
                assert self.end is None or self.here <= self.end, name
                return t

        small = Region((nc.sbuf_base + 63) // 64 * 64)
        ident = small.put("ident", [P, P])
        ones = small.put("ones", [P, P])
        cmask, cmaskR = small.put("cmask", [P, P]), small.put("cmaskR", [P, P], F32R)
        identR = small.put("identR", [P, P], F32R)
        smask = small.put("smask", [NS, NB, NS])
        rs = small.put("rs", [P, 384])
        qr2 = small.put("qr2", [P, 384])
        rope0 = small.here
        cs = small.put("cs", [P, T])
        vgb = Region(rope0).put("vgb", [P, 2, GW])
        rs2 = Region(rope0).put("rs2", [P, T])
        g1, gq, gkv = small.put("g1", [P, KD]), small.put("gq", [P, KQ]), small.put("gkv", [P, KC])
        g_mla, g_gmlp = small.put("g_mla", [P, KG]), small.put("g_gmlp", [P, KG])
        g2, gf = small.put("g2", [P, KD]), small.put("gf", [P, KD])
        bs, bs8 = small.put("bs", [P, G]), small.put("bs8", [NS, G])
        pages = small.put("pages", [1, NB * PAGES], I32)
        epsc, mhalf = small.put("epsc", [P, 1]), small.put("mhalf", [P, 1])
        stat6, mv = small.put("stat6", [P, 2, 6]), small.put("mv", [P, 2, 2])
        ve, rv, ssq = (small.put(n, [P, 4]) for n in ("ve", "rv", "ssq"))
        mx, nmx, sm, rsm = (small.put(n, [P, 4]) for n in ("mx", "nmx", "sm", "rsm"))

        A0 = (small.here + 63) // 64 * 64
        B0 = A0 + 8 * T * KD
        C0 = B0 + 8 * T * KD
        W0 = C0 + 4 * T * KD + 1024
        R0 = W0 + 4 * 4096
        assert R0 + 2 * 4096 <= nc.sbuf_usable_end, (R0 + 8192, nc.sbuf_usable_end)

        raw = Region(R0).put("raw", [P, 2, 1024])
        reg = Region(W0, R0)
        wH, wL = [None, None], [None, None]
        for s in range(2):
            wH[s], wL[s] = reg.put(f"w{s}H", [P, 1024], F32R), reg.put(f"w{s}L", [P, 1024], F32R)

        reg = Region(W0, R0)
        spH, spL = reg.put("spH", [P, G, P], F32R), reg.put("spL", [P, G, P], F32R)
        vt = reg.put("vt", [P, 3, GW])
        wbd = reg.put("wbd", [NS, G, NS])
        reg = Region(A0, B0)
        hH, hL = reg.put("hH", [P, KD, T], F32R), reg.put("hL", [P, KD, T], F32R)
        reg = Region(B0, C0)
        vwH, vwL = reg.put("vwH", [P, KD, GW], F32R), reg.put("vwL", [P, KD, GW], F32R)
        sq0 = Region(reg.here, C0).put("sq0", [P, KD, 384])
        vH, vL = reg.put("vH", [P, NT, GW], F32R), reg.put("vL", [P, NT, GW], F32R)
        mix = Region(B0).put("mix", [P, NT, GW])
        gT = Region(C0 - 4 * KG * T, C0).put("gT", [P, KG, T])
        x1 = Region(C0, W0).put("x1", [P, KD, T])
        reg = Region(C0, W0)
        uwH, uwL = reg.put("uwH", [P, KD, GW], F32R), reg.put("uwL", [P, KD, GW], F32R)

        reg = Region(B0, C0 - 4 * KG * T)
        cqH, cqL = reg.put("cqH", [P, KQ, T], F32R), reg.put("cqL", [P, KQ, T], F32R)
        PT0 = reg.here
        cq = Region(PT0).put("cq", [P, KQ, T])
        pTH, pTL = reg.put("pTH", [P, 4, 512], F32R), reg.put("pTL", [P, 4, 512], F32R)
        PT1 = reg.here
        ckv = reg.put("ckv", [P, KC, T])
        uvH = reg.put("uvH", [P, KC, P], F32R)
        reg = Region(C0, W0)
        sq1 = Region(C0).put("sq1", [P, KQ, 384])
        aT = reg.put("aT", [P, KG, T])
        ckH, ckL = reg.put("ckH", [P, KC, T], F32R), reg.put("ckL", [P, KC, T], F32R)
        uvL = reg.put("uvL", [P, KC, P], F32R)
        reg = Region(A0, B0)
        kH, kL = reg.put("kH", [P, 2, SEQ], F32R), reg.put("kL", [P, 2, SEQ], F32R)
        qH, qL = reg.put("qH", [P, 2, SEQ], F32R), reg.put("qL", [P, 2, SEQ], F32R)
        hvH, hvL = reg.put("hvH", [P, 8, P], F32R), reg.put("hvL", [P, 8, P], F32R)
        prob = reg.put("prob", [P, prob_at(8)])
        KR0 = reg.here
        kr = reg.put("kr", [P, T])
        qt_ = reg.put("qt", [P, 2, 384])
        qs = reg.put("qs", [P, NB, H, TS])

        reg = Region(A0, KR0)
        cp1, cp2 = reg.put("cp1", [P, PAGES, REC]), reg.put("cp2", [P, PAGES, REC])
        cpr = reg.put("cpr", [P, CB, PAGES, PAGE])
        sp = reg.put("sprob", [NS, 2, NEW + NS])
        qlat = reg.put("qlat", [P, KC, 512])
        reg = Region(B0, PT0)
        olat = reg.put("olat", [P, KC, 512])
        cp = [reg.put("cp0", [P, PAGES, REC]), cp1, cp2]
        reg = Region(PT0, PT1)
        ukT, uvr = reg.put("ukT", [NOPE, H, KVR]), reg.put("uvr", [P, KC, GW])
        ctok, spT = reg.put("ctok", [NS, KVR]), reg.put("spT", [P, PAGES + 1, NS])

        reg = Region(A0, B0)
        mH, mL = reg.put("mH", [P, 2 * KG, T], F32R), reg.put("mL", [P, 2 * KG, T], F32R)
        sqm = Region(B0).put("sqm", [P, KG, 384])
        sq2 = Region(B0).put("sq2", [P, 2, T])
        x2 = Region(C0, W0).put("x2", [P, KD, T])
        reg = Region(B0, C0)
        h2H, h2L = reg.put("h2H", [P, KD, T], F32R), reg.put("h2L", [P, KD, T], F32R)
        sq3 = Region(B0).put("sq3", [P, KD, 384])
        reg = Region(A0, B0)
        upH, upL, dnH, dnL = ([reg.put(f"{n}{s}", [P, 1024], F32R) for s in range(2)]
                              for n in ("upH", "upL", "dnH", "dnL"))
        acH, acL = reg.put("acH", [P, 2, T], F32R), reg.put("acL", [P, 2, T], F32R)
        st, av = reg.put("st", [P, 2, 384]), reg.put("av", [P, 2, 384])
        htmp = reg.put("htmp", [P, 4, 384])

        ps = ctx.enter_context(nc.psum_tensor("ps", [P, 8, 512], F32))
        psf = ps[:, :, :].rearrange("p b n -> p (b n)")

        def sem(name):
            return ctx.enter_context(nc.semaphore(name))

        ld_norm1, ld_const, ld_cs, ld_s4 = sem("ld_norm1"), sem("ld_const"), sem("ld_cs"), sem("ld_s4")
        ld_x = [sem(f"ld_x{c}") for c in range(NC)]
        ld_x2 = [sem(f"ld_x2_{j}") for j in range(4)]
        raw_full = [sem(f"raw_full{s}") for s in range(2)]
        cp_full = [sem(f"cp_full{s}") for s in range(CB)]
        out_v, out_ckv, out_kr, out_y = sem("out_v"), sem("out_ckv"), sem("out_kr"), sem("out_y")
        made, made_r, sp_masked, split_seen, split_hi, split_lo = (
            sem(n) for n in ("made", "made_r", "sp_masked", "split_seen", "split_hi", "split_lo"))
        n1_sq, n1_ss, n1_std, n1_inv, n1_x, n1_hi, n1_lo = (
            sem("n1_" + n) for n in ("sq", "ss", "std", "inv", "x", "hi", "lo"))
        v_ready, v_gelu, v_b1, v_b2, v_ve, v_rv, v_n1, v_n2, v_fin, v_hi, v_lo = (
            sem("v_" + n) for n in ("ready", "gelu", "b1", "b2", "ve", "rv", "n1", "n2", "fin", "hi", "lo"))
        sp_ready, sp_free = sem("sp_ready"), sem("sp_free")
        u_ready, u_gelu, u_g, u_sq, u_ve, u_rv, u_gn, u_tr, u_out = (
            sem("u_" + n) for n in ("ready", "gelu", "g", "sq", "ve", "rv", "gn", "tr", "out"))
        z_ready, z_free = sem("z_ready"), sem("z_free")
        kr_a, kr_ok, kr_hi, kr_lo = sem("kr_a"), sem("kr_ok"), sem("kr_hi"), sem("kr_lo")
        n2_sq, n2_ss, n2_std, n2_inv, n2_x, n2_hi, n2_lo = (
            sem("n2_" + n) for n in ("sq", "ss", "std", "inv", "x", "hi", "lo"))
        gen_ready, gen_free, gen_hi = sem("gen_ready"), sem("gen_free"), sem("gen_hi")
        q_nope, q_cos, q_rope, q_hi, q_lo, q_s = (
            sem("q_" + n) for n in ("nope", "cos", "rope", "hi", "lo", "s"))
        vg_ready, vg_hi, vg_free = sem("vg_ready"), sem("vg_hi"), sem("vg_free")
        s_ready, s_mx, s_nm, s_exp, s_rc, s_pn, s_pd = (
            sem("s_" + n) for n in ("ready", "mx", "nm", "exp", "rc", "pn", "pd"))
        t_ready, t_hi, t_free, pv_x, o_free = (sem(n) for n in ("t_ready", "t_hi", "t_free", "pv_x", "o_free"))
        q4_ready, q4_e = sem("q4_ready"), sem("q4_e")
        s4_ready, s4_mk, s4_mx, s4_nm, s4_exp, s4_rc, s4_n = (
            sem("s4_" + n) for n in ("ready", "mk", "mx", "nm", "exp", "rc", "n"))
        t4_ready, t4_a, t4_b, pv4, o4, a4, a4_e = (
            sem(n) for n in ("t4_ready", "t4_a", "t4_b", "pv4", "o4", "a4", "a4_e"))
        n3_sq, n3_ss, n3_std, n3_inv, n3_x = (sem("n3_" + n) for n in ("sq", "ss", "std", "inv", "x"))
        m_hi, m_lo, w_ready, w_free = sem("m_hi"), sem("m_lo"), sem("w_ready"), sem("w_free")
        n4_sq, n4_ss, n4_std, n4_inv = (sem("n4_" + n) for n in ("sq", "ss", "std", "inv"))
        h2_x, h2_hi, h2_lo = sem("h2_x"), sem("h2_hi"), sem("h2_lo")
        gu_ready, f_silu, f_act, f_hi, f_lo, dn_ready, y_free = (
            sem(n) for n in ("gu_ready", "f_silu", "f_act", "f_hi", "f_lo", "dn_ready", "y_free"))
        n5_sq, n5_ss, n5_std, n5_inv, n5_x = (sem("n5_" + n) for n in ("sq", "ss", "std", "inv", "x"))

        norm1_loads = [(g1, "g1")]
        const_loads = [(ident, "ident"), (vgb, "vgb"), (wbd, "wbd"), (bs, "bs"), (bs8, "bs8"),
                       (gq, "gq"), (gkv, "gkv"), (cmask, "cmask"), (smask, "smask"),
                       (g_mla, "g_mla"), (g_gmlp, "g_gmlp"), (g2, "g2"), (gf, "gf"), (pages, "pages")]
        CONST = 16 * len(const_loads)

        block = ctx.enter_context(nc.Block())

        @block.sync
        def _(sp_):
            def piece(n, src, width=1024):
                if n >= 2:
                    sp_.wait_ge(split_lo, n - 1)
                sp_.dma_start(raw[:, n % 2, 0:width], src).then_inc(raw_full[n % 2], 16)

            for c, (c0, n) in enumerate(CH):
                sp_.dma_start(x1[:, :, c0:c0 + n], d["x"][:, :, c0:c0 + n]).then_inc(ld_x[c], 16)
                if c == 0:
                    sp_.dma_start(g1[:, :], d["g1"]).then_inc(ld_norm1, 16)
                    piece(N_V, d["w_v"][0])
                    piece(N_V + 1, d["w_v"][1])
            for t, name in const_loads:
                full = tuple(slice(None) for _ in t.shape)
                sp_.dma_start(t[full], d[name]).then_inc(ld_const, 16)
            for j in range(2, 4):
                piece(N_V + j, d["w_v"][j])
            piece(N_SP, d["w_sp"])
            for j in range(4):
                piece(N_U + j, d["w_u"][j])
            sp_.wait_ge(v_fin, NT)
            sp_.dma_start(d["v_out"], vt[0:NS, 2, :]).then_inc(out_v, 16)
            sp_.dma_start(cs[:, :], d["cs"]).then_inc(ld_cs, 16)
            for m in range(KQ + KC + 1):
                piece(N_IN + m, d["w_in"][m])
            for p in range(PAIRS):
                piece(N_HEAD + 2 * p, d["w_qk"][p])
                piece(N_HEAD + 2 * p + 1, d["w_uv"][p], KC * P)
                if p == 0:
                    sp_.wait_ge(n2_x, KQ * NC + KC * NC)
                    sp_.dma_start(d["ckv_out"], ckv[:, :, :]).then_inc(out_ckv, 16)
                    sp_.wait_ge(kr_ok, NC)
                    sp_.dma_start(d["kr_out"], kr[NOPE:QK, :]).then_inc(out_kr, 16)
            for m in range(2):
                piece(N_OUT + m, d["w_out"][m])

            def fetch(b, latents, ropes):
                for j in range(PAGES):
                    page = sp_.value_load(pages[0:1, b * PAGES + j:b * PAGES + j + 1],
                                          min_val=0, max_val=POOL - 1)
                    if latents:
                        src = d["cache"][bass.ds(page, 1), :, :].rearrange("a p n -> (a p) n")
                        sp_.dma_start(cp[b % CB][:, j, :], src).then_inc(cp_full[b % CB], 16)
                    if ropes:
                        src = d["cache_r"][bass.ds(page, 1), :, :].rearrange("a p n -> (a p) n")
                        sp_.dma_start(cpr[NOPE:QK, b % CB, j, :], src).then_inc(cp_full[b % CB], 16)

            sp_.wait_ge(gen_ready, GEN * PAIRS)
            sp_.wait_ge(ld_const, CONST)
            fetch(0, True, False)
            sp_.wait_ge(pv_x, tr_count(UNITS))
            sp_.dma_start(ukT[:, :, :], d["w_ukT"]).then_inc(ld_s4, 16)
            fetch(0, False, True)
            sp_.dma_start(uvr[:, :, :], d["w_uvr"]).then_inc(ld_s4, 16)
            for b in range(1, NB):
                if b >= CB:
                    sp_.wait_ge(pv4, b - CB + 1)
                fetch(b, True, True)
            sp_.wait_ge(m_lo, KG + KG * NC)
            for j in range(4):
                sp_.dma_start(x2[:, 2 * j:2 * j + 2, :], d["x"][:, 2 * j:2 * j + 2, :]).then_inc(ld_x2[j], 16)
            for m in range(2, KD):
                piece(N_OUT + m, d["w_out"][m])
            with sp_.Fori(0, NF // 2) as i:
                for j in range(BODY):
                    n = N_FF + j
                    sp_.wait_ge(split_lo, BODY * i + (n - 1))
                    src = d["w_ff"][bass.ds(BODY * i + j, 1), :, :].rearrange("a p n -> (a p) n")
                    sp_.dma_start(raw[:, n % 2, :], src).then_inc(raw_full[n % 2], 16)
            for c, (c0, n) in enumerate(CH):
                sp_.wait_ge(n5_x, KD * (c + 1))
                sp_.dma_start(d["y"][:, :, c0:c0 + n], x2[:, :, c0:c0 + n]).then_inc(out_y, 16)
            sp_.wait_ge(out_v, 16)
            sp_.wait_ge(out_ckv, 16)
            sp_.wait_ge(out_kr, 16)
            sp_.wait_ge(out_y, 16 * NC)

        @block.gpsimd
        def _(pool):
            def split(n, hi, lo, width=1024, turns=0, i=0):
                r = raw[:, n % 2, 0:width]
                pool.wait_ge(raw_full[n % 2], 16 * (n // 2 + 1) + 8 * turns * i)
                if turns:
                    pool.sem_inc(split_seen, 1)
                pool.tensor_scalar(hi, r, 1.0, 0.0, ALU.mult, ALU.add).then_inc(split_hi, 1)
                pool.wait_ge(split_hi, n + 1 + turns * i)
                pool.tensor_tensor(lo, r, hi, ALU.subtract).then_inc(split_lo, 1)

            def gw(t, j):
                return t[:, 2 * j:2 * j + 2, :].rearrange("p k n -> p (k n)")

            pool.memset(ones[:, :], 1.0).then_inc(made, 1)
            pool.memset(epsc[:, :], EPS).then_inc(made, 1)
            pool.memset(mhalf[:, :], -0.5).then_inc(made, 1)
            for j in range(4):
                split(N_V + j, gw(vwH, j), gw(vwL, j))
            pool.wait_ge(raw_full[N_SP % 2], 16 * (N_SP // 2 + 1))
            rsp = raw[:, N_SP % 2, :].rearrange("p (g i) -> p g i", g=G)
            pool.affine_select(out=rsp, in_=rsp, compare_op=ALU.is_ge, fill=0.0, base=0,
                               pattern=[[0, G], [1, P]], channel_multiplier=-1).then_inc(sp_masked, 1)
            pool.wait_ge(ld_const, CONST)
            pool.affine_select(out=wbd[:, :, :], in_=wbd[:, :, :], compare_op=ALU.is_ge, fill=0.0, base=0,
                               pattern=[[0, G], [1, NS]], channel_multiplier=-1).then_inc(sp_masked, 1)
            pool.wait_ge(sp_masked, 2)
            flat = "p g i -> p (g i)"
            split(N_SP, spH[:, :, :].rearrange(flat), spL[:, :, :].rearrange(flat))
            pool.wait_ge(made, 3)
            for t in range(NT):
                m, s = rows(t), t % 4
                pool.wait_ge(v_ve, t + 1)
                pool.tensor_tensor(rv[0:m, s:s + 1], ve[0:m, s:s + 1], mhalf[0:m, :], ALU.pow).then_inc(v_rv, 1)
                if t % 2:
                    pool.wait_ge(n1_lo, KD * NC)
                    j = t // 2
                    split(N_U + j, gw(uwH, j), gw(uwL, j))
                if t < NT - 1:
                    pool.wait_ge(v_hi, t + 1)
                    pool.tensor_tensor(vL[:, t, :], vt[:, t % 2, :], vH[:, t, :], ALU.subtract).then_inc(v_lo, 1)

            def in_piece(m):
                split(N_IN + m, wH[m % 2][:, :], wL[m % 2][:, :])

            for t in range(NT):
                m, s = rows(t), t % 4
                pool.wait_ge(u_ve, t + 1)
                pool.tensor_tensor(rv[0:m, s:s + 1], ve[0:m, s:s + 1], mhalf[0:m, :], ALU.pow).then_inc(u_rv, 1)
                if t == 2:
                    pool.wait_ge(sp_ready, G + 1)
                    in_piece(0)
            pool.wait_ge(u_sq, NT)
            pool.wait_ge(u_g, NT)
            pool.wait_ge(out_v, 16)
            in_piece(1)
            for m in range(2, KQ + KC + 1):
                pool.wait_ge(z_ready, NC * (m - 1))
                in_piece(m)

            def head_pieces(p):
                if p < 2:
                    pool.wait_ge(z_ready, NC * (KQ + KC + 1 if p else KQ + KC))
                else:
                    pool.wait_ge(gen_ready, GEN * (p - 1))
                split(N_HEAD + 2 * p, wH[p % 2][:, :], wL[p % 2][:, :])
                if p:
                    pool.wait_ge(vg_ready, 2 * p)
                flat = "p k n -> p (k n)"
                split(N_HEAD + 2 * p + 1, uvH[:, :, :].rearrange(flat), uvL[:, :, :].rearrange(flat), KC * P)

            def query_lo(p):
                for hh in range(2):
                    for c, (c0, n) in enumerate(CH):
                        j = 2 * NC * p + NC * hh + c
                        n = min(n, SEQ - c0)
                        pool.wait_ge(q_hi, j + 1)
                        pool.tensor_tensor(qL[0:QK, hh, c0:c0 + n], qt_[0:QK, j % 2, 0:n],
                                           qH[0:QK, hh, c0:c0 + n], ALU.subtract).then_inc(q_lo, 1)

            def normalise(u):
                for qi in range(3):
                    r, qt = 4 * u + qi, 4 * (u % 2) + qi
                    n = P * (qt + 1)
                    row = prob[:, prob_at(qt):prob_at(qt) + n]
                    pool.wait_ge(s_rc, r + 1)
                    pool.tensor_tensor(row, row, rsm[:, r % 4:r % 4 + 1].broadcast_to((P, n)),
                                       ALU.mult).then_inc(s_pn, 1)

            head_pieces(0)
            query_lo(0)
            head_pieces(1)
            normalise(0)
            for u in range(UNITS):
                p = u // 4
                if u % 4 == 3 and u < UNITS - 1:
                    query_lo(p + 1)
                if u < UNITS - 1:
                    normalise(u + 1)
                if u % 4 == 3 and p + 2 < PAIRS:
                    head_pieces(p + 2)
            for m in range(KD):
                if m < 2:
                    pool.wait_ge(gen_ready, GEN * PAIRS)
                else:
                    pool.wait_ge(w_ready, NC * (m - 1))
                split(N_OUT + m, wH[m % 2][:, :], wL[m % 2][:, :])

            def ff_pieces(first, i, after_h2):
                for s in range(2):
                    if first:
                        pool.wait_ge(w_ready, NC * KD)
                    else:
                        pool.wait_ge(gu_ready, 2 * NC * i + (NC * (s - 1)))
                    n = N_FF + 2 * s
                    split(n, wH[s][:, :], wL[s][:, :], turns=BODY, i=i)
                    split(n + 1, upH[s][:, :], upL[s][:, :], turns=BODY, i=i)
                    if first and s == 0:
                        after_h2()
                if not first:
                    pool.wait_ge(dn_ready, NC * KD * i)
                for s in range(2):
                    split(N_FF + 4 + s, dnH[s][:, :], dnL[s][:, :], turns=BODY, i=i)

            def h2_lows():
                for c, (c0, n) in enumerate(CH):
                    for k in range(KD):
                        j = KD * c + k
                        pool.wait_ge(h2_hi, j + 1)
                        pool.tensor_tensor(h2L[:, k, c0:c0 + n], htmp[:, j % 4, 0:n], h2H[:, k, c0:c0 + n],
                                           ALU.subtract).then_inc(h2_lo, 1)

            ff_pieces(True, 0, h2_lows)
            with pool.Fori(1, NF // 2) as i:
                ff_pieces(False, i, None)

        @block.tensor
        def _(pe):
            def mm3(out, wh, wl, xh, xl, start, stop):
                nc.tensor.matmul(out, wh, xh, start=start, stop=False)
                nc.tensor.matmul(out, wh, xl, start=False, stop=False)
                return nc.tensor.matmul(out, wl, xh, start=False, stop=stop)

            def sum_squares(out, sq, k):
                for j in range(k):
                    m = nc.tensor.matmul(out, ones[:, :], sq[:, j, :], start=j == 0, stop=j == k - 1)
                return m

            pe.wait_ge(made, 1)
            for c, (c0, n) in enumerate(CH):
                pe.wait_ge(n1_sq, c + 1)
                sum_squares(ps[:, 4 + c, 0:n], sq0[:, :, 0:n], KD).then_inc(n1_ss, 1)

            pe.wait_ge(split_lo, N_SP)
            for t in range(NT):
                m, b = rows(t), t % 4
                pe.wait_ge(n1_lo, KD * (t // 3 + 1))
                if t >= 4:
                    pe.wait_ge(v_gelu, t - 3)
                cols = slice(P * t, P * t + m)
                for k in range(KD):
                    last = mm3(ps[0:m, b, :], hH[:, k, cols], hL[:, k, cols], vwH[:, k, :], vwL[:, k, :],
                               k == 0, k == KD - 1)
                last.then_inc(v_ready, 1)
            pe.wait_ge(split_lo, N_U)
            pe.wait_ge(v_lo, NT - 1)
            for g in range(G):
                b = 4 + g % 4
                if g >= 4:
                    pe.wait_ge(sp_free, g - 3)
                else:
                    pe.wait_ge(n1_std, NC)
                out = ps[:, b, :].rearrange("p (c n) -> p c n", c=8)
                cols = slice(GD * g, GD * g + GD)
                mm3(out, spH[:, g, :], spL[:, g, :], vH[:, 0:8, cols], vL[:, 0:8, cols],
                    True, True).then_inc(sp_ready, 1)
            pe.wait_ge(v_fin, NT)
            pe.wait_ge(sp_masked, 2)
            pe.wait_ge(sp_free, 5)
            for g in range(G):
                last = nc.tensor.matmul(ps[0:NS, 4, GD * g:GD * g + GD], wbd[:, g, :],
                                        vt[0:NS, 2, GD * g:GD * g + GD], start=True, stop=True)
            last.then_inc(sp_ready, 1)
            pe.wait_ge(v_gelu, NT)
            pe.wait_ge(split_lo, N_IN)
            for t in range(NT + 2):
                if t < NT:
                    m, b = rows(t), t % 4
                    if t >= 4:
                        pe.wait_ge(u_gelu, t - 3)
                    cols = slice(P * t, P * t + m)
                    for k in range(KD):
                        last = mm3(ps[0:m, b, :], hH[:, k, cols], hL[:, k, cols], uwH[:, k, :], uwL[:, k, :],
                                   k == 0, k == KD - 1)
                    last.then_inc(u_ready, 1)
                if t >= 2:
                    w = t - 2
                    m, b = rows(w), 5 + w % 2
                    pe.wait_ge(u_gn, w + 1)
                    if w >= 2:
                        pe.wait_ge(u_out, w - 1)
                    else:
                        pe.wait_ge(sp_free, G + 1)
                    for j in range(KG):
                        last = nc.tensor.transpose(ps[:, b, P * j:P * j + m], mix[0:m, w, P * j:P * j + P],
                                                   ident[0:m, 0:m])
                    last.then_inc(u_tr, 1)
            pe.wait_ge(u_gelu, NT)
            sums = {11: 0, 12: 1, 13: 2, 15: 3, 16: 4, 17: 5}
            for m in range(KQ + KC + 1):
                pe.wait_ge(split_lo, N_IN + m + 1)
                s = m % 2
                for c, (c0, n) in enumerate(CH):
                    q = NC * m + c
                    if q >= 4:
                        pe.wait_ge(z_free, q - 3)
                    for k in range(KD):
                        w = slice(P * k, P * k + P)
                        last = mm3(ps[:, q % 4, 0:n], wH[s][:, w], wL[s][:, w], hH[:, k, c0:c0 + n],
                                   hL[:, k, c0:c0 + n], k == 0, k == KD - 1)
                    last.then_inc(z_ready, 1)
                    if q in sums:
                        j = sums[q]
                        nj = CH[j % NC][1]
                        pe.wait_ge(n2_sq, j + 1)
                        if j < 3:
                            pe.wait_ge(u_out, NT)
                        else:
                            pe.wait_ge(n2_std, j - 2)
                        sum_squares(ps[:, 4 + j % NC, 0:nj], sq1[:, :, 0:nj], KQ if j < NC else KC).then_inc(n2_ss, 1)

            def query_key(p, i):
                s = p % 2
                if i == 0:
                    pe.wait_ge(split_lo, N_HEAD + 2 * p + 1)
                    if p == 0:
                        pe.wait_ge(n2_lo, NC)
                        pe.wait_ge(z_free, NC * (KQ + KC))
                        pe.wait_ge(kr_ok, NC)
                    else:
                        pe.wait_ge(s_exp, 16 * p)
                if i >= 4:
                    pe.wait_ge(gen_free, GEN * p + i - 3)
                if i < 2 * NC:
                    hh, (c0, n) = i // NC, CH[i % NC]
                    for k in range(KQ):
                        w = slice(256 * k + P * hh, 256 * k + P * hh + P)
                        last = mm3(ps[:, i % 4, 0:n], wH[s][:, w], wL[s][:, w], cqH[:, k, c0:c0 + n],
                                   cqL[:, k, c0:c0 + n], k == 0, k == KQ - 1)
                else:
                    if i == 2 * NC:
                        pe.wait_ge(n2_lo, 2 * NC)
                    c0 = 512 * (i - 2 * NC)
                    for k in range(KC):
                        w = slice(768 + P * k, 768 + P * k + P)
                        last = mm3(ps[:, i % 4, :], wH[s][:, w], wL[s][:, w], ckH[:, k, c0:c0 + 512],
                                   ckL[:, k, c0:c0 + 512], k == 0, k == KC - 1)
                last.then_inc(gen_ready, 1)

            def values(p):
                if p:
                    pe.wait_ge(t_free, tr_count(4 * p))
                else:
                    pe.wait_ge(n2_std, 2 * NC)
                pe.wait_ge(split_lo, N_HEAD + 2 * p + 2)
                for j in range(2):
                    for x in range(4):
                        cols = slice(P * (4 * j + x), P * (4 * j + x) + P)
                        for k in range(KC):
                            last = mm3(ps[:, 4 + j, P * x:P * x + P], ckH[:, k, cols], ckL[:, k, cols],
                                       uvH[:, k, :], uvL[:, k, :], k == 0, k == KC - 1)
                    last.then_inc(vg_ready, 1)

            def score(u, qi):
                p, hh, blk = u // 4, u // 2 % 2, u % 2
                if qi == 0:
                    pe.wait_ge(q_lo, 2 * NC * p + NC * (hh + 1))
                    pe.wait_ge(gen_free, GEN * (p + 1))
                if u == 0 and qi == 0:
                    pe.wait_ge(kr_lo, 2)
                    pe.wait_ge(made_r, 2)
                r, qt = 4 * u + qi, 4 * blk + qi
                if r >= 2:
                    pe.wait_ge(s_exp, r - 1)
                q = slice(P * qt, P * qt + P)
                for c0 in range(0, P * (qt + 1), 512):
                    n = min(512, P * (qt + 1) - c0)
                    out = ps[:, 2 * (r % 2) + c0 // 512, :]
                    last = mm3(out[:, 0:n], qH[0:QK, hh, q], qL[0:QK, hh, q], kH[0:QK, hh, c0:c0 + n],
                               kL[0:QK, hh, c0:c0 + n], True, c0 + n <= P * qt)
                last = nc.tensor.matmul(out[:, n - P:n], identR[:, :], cmaskR[:, :], start=False, stop=True)
                last.then_inc(s_ready, 1)

            def weigh(u):
                blk = u % 2
                nk = 4 * (blk + 1)

                def turn(kt):
                    x = tr_count(u) + kt
                    if x >= 2:
                        pe.wait_ge(t_free, x - 1)
                    for qi in range(max(0, kt - 4 * blk), 4):
                        at = prob_at(4 * blk + qi) + P * kt
                        last = nc.tensor.transpose(ps[:, 4 + x % 2, P * qi:P * qi + P], prob[:, at:at + P],
                                                   ident[:, :])
                    last.then_inc(t_ready, 1)

                def product(kt):
                    x = tr_count(u) + kt
                    c0 = P * max(0, kt - 4 * blk)
                    pe.wait_ge(t_free, x + 1)
                    if kt == 0 and u >= 2:
                        pe.wait_ge(o_free, u - 1)
                    mm3(ps[:, 6 + u % 2, c0:512], hvH[:, kt, :], hvL[:, kt, :], pTH[:, x % 4, c0:512],
                        pTL[:, x % 4, c0:512], kt == 0, kt == nk - 1).then_inc(pv_x, 1)

                for kt in range(nk + 2):
                    for i in gens_at(u, kt):
                        query_key(u // 4 + 1, i)
                    if (qi := row_at(u, kt)) is not None:
                        score(u + 1, qi)
                    if kt == 0:
                        pe.wait_ge(s_pn, 3 * u + 3)
                        pe.wait_ge(s_pd, u + 1)
                        pe.wait_ge(vg_free, 2 * (u // 4 + 1))
                    if kt < nk:
                        turn(kt)
                    if kt >= 2:
                        product(kt - 2)

            for i in range(GEN):
                query_key(0, i)
            values(0)
            for qi in range(4):
                score(0, qi)
            for u in range(UNITS):
                p = u // 4
                weigh(u)
                if u % 4 == 3 and u < UNITS - 1:
                    values(p + 1)

            pe.wait_ge(ld_s4, 32)
            pe.wait_ge(q_s, H)
            pe.wait_ge(s_exp, 4 * UNITS)
            for r in range(KC):
                for h in range(H):
                    last = nc.tensor.matmul(ps[:, r, NS * h:NS * h + NS], ukT[:, h, P * r:P * r + P],
                                            qs[0:NOPE, :, h, :], start=True, stop=True)
            last.then_inc(q4_ready, 1)
            for r in range(KC):
                last = nc.tensor.transpose(ps[0:NS, 2, P * r:P * r + P], ckv[:, r, SEQ:T], ident[:, :])
            last.then_inc(q4_ready, 1)

            def sample_scores(b):
                pe.wait_ge(cp_full[b % CB], 2 * 16 * PAGES * (b // CB + 1))
                if b == 0:
                    pe.wait_ge(q4_e, 3)
                elif b == 1:
                    pe.wait_ge(t_free, tr_count(UNITS))
                else:
                    pe.wait_ge(s4_exp, b - 1)
                    pe.wait_ge(t4_b, b - 1)
                q = slice(NS * b, NS * b + NS)
                for part in range(3):
                    bank = 3 * (b % 2) + part
                    for r in range(3):
                        w = qlat[:, r, q] if r < 2 else qs[NOPE:QK, b, :, :].rearrange("p h t -> p (h t)")
                        if part < 2:
                            pg = slice(4 * part, 4 * part + 4)
                            x = cp[b % CB][:, pg, P * r:P * r + P] if r < 2 else cpr[NOPE:QK, b % CB, pg, :]
                            out = ps[0:NS, bank, :].rearrange("p (g n) -> p g n", g=4)
                        else:
                            x = ckv[:, r, SEQ:T] if r < 2 else kr[NOPE:QK, SEQ:T]
                            out = ps[0:NS, bank, 0:NS]
                        last = nc.tensor.matmul(out, w, x, start=r == 0, stop=r == 2)
                last.then_inc(s4_ready, 1)

            sample_scores(0)
            for b in range(NB):
                if b + 1 < NB:
                    sample_scores(b + 1)
                pe.wait_ge(s4_n, b + 1)
                if b:
                    pe.wait_ge(t4_a, b)
                else:
                    pe.wait_ge(o_free, UNITS)
                for j in range(PAGES):
                    nc.tensor.transpose(ps[:, 6, NS * j:NS * j + NS], sp[:, b % 2, P * j:P * j + P],
                                        ident[0:NS, 0:NS])
                nc.tensor.transpose(ps[0:NS, 3 * (b % 2) + 2, NS:2 * NS], sp[:, b % 2, NEW:NEW + NS],
                                    ident[0:NS, 0:NS]).then_inc(t4_ready, 1)
                pe.wait_ge(t4_a, b + 1)
                pe.wait_ge(t4_b, b + 1)
                if b:
                    pe.wait_ge(o4, b)
                for r in range(KC):
                    out = ps[:, 7, NS * r:NS * r + NS]
                    for j in range(PAGES):
                        nc.tensor.matmul(out, cp[b % CB][:, j, KVR + P * r:KVR + P * r + P], spT[:, j, :],
                                         start=j == 0, stop=False)
                    last = nc.tensor.matmul(out, ctok[:, P * r:P * r + P], spT[0:NS, PAGES, :],
                                            start=False, stop=True)
                last.then_inc(pv4, 1)
            pe.wait_ge(o4, NB)
            pe.wait_ge(s4_exp, NB)
            for h in range(H):
                out = ps[VH * (h % 2):VH * (h % 2) + VH, 0, NS * (h // 2):NS * (h // 2) + NS]
                for r in range(KC):
                    last = nc.tensor.matmul(out, uvr[:, r, VH * h:VH * h + VH], olat[:, r, NS * h:NS * h + NS],
                                            start=r == 0, stop=r == KC - 1)
            last.then_inc(a4, 1)

            for c, (c0, n) in enumerate(CH):
                pe.wait_ge(n3_sq, c + 1)
                sum_squares(ps[:, 4 + c, 0:n], sqm[:, :, 0:n], KG).then_inc(n3_ss, 1)
            pe.wait_ge(m_lo, KG + KG * NC)

            def sum_x2(j):
                pe.wait_ge(n4_sq, j + 1)
                for c, (c0, n) in enumerate(CH):
                    last = nc.tensor.matmul(ps[:, 4 + c, 0:n], ones[:, :], sq2[:, j % 2, c0:c0 + n],
                                            start=j == 0, stop=j == KD - 1)
                last.then_inc(n4_ss, 1)

            for m in range(KD):
                s = m % 2
                pe.wait_ge(split_lo, N_OUT + m + 1)
                for c, (c0, n) in enumerate(CH):
                    q = NC * m + c
                    if q >= 4:
                        pe.wait_ge(w_free, q - 3)
                    for k in range(2 * KG):
                        w = slice(P * k, P * k + P)
                        last = mm3(ps[:, q % 4, 0:n], wH[s][:, w], wL[s][:, w], mH[:, k, c0:c0 + n],
                                   mL[:, k, c0:c0 + n], k == 0, k == 2 * KG - 1)
                    last.then_inc(w_ready, 1)
                if m >= 1:
                    sum_x2(m - 1)
            sum_x2(KD - 1)

            def feed_forward(first, i):
                for s in range(2):
                    pe.wait_ge(split_lo, N_FF + 2 * s + 2 + BODY * i)
                    for c, (c0, n) in enumerate(CH):
                        q = NC * s + c
                        g0 = 2 * (q % 2)
                        if first and s == 0:
                            pe.wait_ge(h2_lo, KD * (c + 1))
                        if first and q < 2:
                            pe.wait_ge(w_free, NC * KD)
                        else:
                            pe.wait_ge(f_act, 2 * NC * i + (q - 1))
                        for hi, lo, b in ((wH, wL, g0), (upH, upL, g0 + 1)):
                            for k in range(KD):
                                w = slice(P * k, P * k + P)
                                last = mm3(ps[:, b, 0:n], hi[s][:, w], lo[s][:, w], h2H[:, k, c0:c0 + n],
                                           h2L[:, k, c0:c0 + n], k == 0, k == KD - 1)
                        last.then_inc(gu_ready, 1)
                pe.wait_ge(split_lo, N_FF + BODY + BODY * i)
                for c, (c0, n) in enumerate(CH):
                    pe.wait_ge(f_lo, 2 * NC * i + (NC + c + 1))
                    for m in range(KD):
                        r = KD * c + m
                        if first and r < 4:
                            pe.wait_ge(n4_std, NC)
                        else:
                            pe.wait_ge(y_free, NC * KD * i + (r - 3))
                        w = slice(P * m, P * m + P)
                        for s in range(2):
                            last = mm3(ps[:, 4 + r % 4, 0:n], dnH[s][:, w], dnL[s][:, w], acH[:, s, c0:c0 + n],
                                       acL[:, s, c0:c0 + n], s == 0, s == 1)
                        last.then_inc(dn_ready, 1)

            feed_forward(True, 0)
            with pe.Fori(1, NF // 2) as i:
                feed_forward(False, i)
            pe.wait_ge(f_act, NC * NF)
            for c, (c0, n) in enumerate(CH):
                pe.wait_ge(n5_sq, c + 1)
                sum_squares(ps[:, c, 0:n], sq3[:, :, 0:n], KD).then_inc(n5_ss, 1)

        @block.scalar
        def _(act):
            def root(out, sums, width):
                return nc.scalar.activation(out, sums, ACT.Sqrt, bias=epsc[:, :], scale=1.0 / width)

            def hi(out, x, scale=1.0):
                return nc.scalar.activation(out, x, ACT.Copy, scale=scale)

            def squares1(c):
                c0, n = CH[c]
                act.wait_ge(ld_x[c], 16)
                if c:
                    act.wait_ge(n1_ss, c)
                nc.scalar.activation(sq0[:, :, 0:n], x1[:, :, c0:c0 + n], ACT.Square).then_inc(n1_sq, 1)

            act.wait_ge(made, 2)
            squares1(0)
            for c, (c0, n) in enumerate(CH):
                act.wait_ge(n1_ss, c + 1)
                if c:
                    act.wait_ge(n1_x, KD * c)
                root(rs[:, 0:n], ps[:, 4 + c, 0:n], D).then_inc(n1_std, 1)
                if c + 1 < NC:
                    squares1(c + 1)
                for k in range(KD):
                    act.wait_ge(n1_x, KD * c + k + 1)
                    hi(hH[:, k, c0:c0 + n], x1[:, k, c0:c0 + n]).then_inc(n1_hi, 1)

            act.wait_ge(ld_const, CONST)
            hi(cmaskR[:, :], cmask[:, :]).then_inc(made_r, 1)
            hi(identR[:, :], ident[:, :]).then_inc(made_r, 1)
            for t in range(NT + 1):
                if t < NT:
                    m, slot = rows(t), 2 if t == NT - 1 else t % 2
                    act.wait_ge(v_ready, t + 1)
                    if t >= 2:
                        act.wait_ge(v_lo, t - 1)
                    nc.scalar.activation(vt[0:m, slot, :], ps[0:m, t % 4, :], ACT.Gelu).then_inc(v_gelu, 1)
                if 1 <= t < NT:
                    if t == 1:
                        act.wait_ge(n1_ss, NC)
                    act.wait_ge(v_fin, t)
                    hi(vH[:, t - 1, :], vt[:, (t - 1) % 2, :]).then_inc(v_hi, 1)
            act.wait_ge(v_lo, NT - 1)
            for t in range(NT + 2):
                if t < NT:
                    m = rows(t)
                    act.wait_ge(u_ready, t + 1)
                    if t >= 2:
                        act.wait_ge(u_sq, t - 1)
                    nc.scalar.activation(vt[0:m, t % 2, :], ps[0:m, t % 4, :], ACT.Gelu).then_inc(u_gelu, 1)
                if 1 <= t <= NT:
                    w = t - 1
                    m, s = rows(w), w % 4
                    act.wait_ge(u_g, w + 1)
                    nc.scalar.activation(vt[0:m, w % 2, :], mix[0:m, w, :], ACT.Square,
                                         accum_out=ssq[0:m, s:s + 1]).then_inc(u_sq, 1)
                if t >= 2:
                    w = t - 2
                    m = rows(w)
                    act.wait_ge(u_tr, w + 1)
                    hi(gT[:, :, P * w:P * w + m],
                       ps[:, 5 + w % 2, :].rearrange("p (k n) -> p k n", k=KG)[:, :, 0:m]).then_inc(u_out, 1)

            def move(q):
                c0, n = CH[q % NC]
                m = q // NC
                out = cq[:, m, c0:c0 + n] if m < KQ else ckv[:, m - KQ, c0:c0 + n]
                act.wait_ge(z_ready, q + 1)
                hi(out, ps[:, q % 4, 0:n]).then_inc(z_free, 1)

            def squares2(j):
                c0, n = CH[j % NC]
                k, x = (KQ, cq) if j < NC else (KC, ckv)
                act.wait_ge(z_free, NC * (KQ - 1) + j + 1 if j < NC else NC * (KQ + KC - 1) + j - NC + 1)
                if j:
                    act.wait_ge(n2_ss, j)
                nc.scalar.activation(sq1[:, 0:k, 0:n], x[:, :, c0:c0 + n], ACT.Square).then_inc(n2_sq, 1)

            def root2(j):
                n = CH[j % NC][1]
                act.wait_ge(n2_ss, j + 1)
                if j:
                    act.wait_ge(n2_x, KQ * j if j <= NC else KQ * NC + KC * (j - NC))
                root(rs[:, 0:n], ps[:, 4 + j % NC, 0:n], QR if j < NC else KVR).then_inc(n2_std, 1)

            def hi2(j):
                c0, n = CH[j % NC]
                act.wait_ge(n2_x, KQ * (j + 1) if j < NC else KQ * NC + KC * (j - NC + 1))
                out, x = (cqH, cq) if j < NC else (ckH, ckv)
                hi(out[:, :, c0:c0 + n], x[:, :, c0:c0 + n]).then_inc(n2_hi, 1)

            act.wait_ge(u_ready, NT)
            act.wait_ge(u_tr, NT)
            for q in range(9):
                move(q)
            squares2(0)
            for q in (9, 10, 11):
                move(q)
            root2(0)
            squares2(1)
            move(12)
            root2(1)
            squares2(2)
            move(13)
            root2(2)
            move(14)
            squares2(3)
            for j in range(NC):
                hi2(j)
            root2(3)
            squares2(4)
            root2(4)
            squares2(5)
            root2(5)
            for j in range(NC, 2 * NC):
                hi2(j)
            act.wait_ge(kr_ok, NC)
            for hh in range(2):
                hi(kH[NOPE:QK, hh, :], kr[NOPE:QK, 0:SEQ]).then_inc(kr_hi, 1)

            def move_gen(p, i):
                act.wait_ge(gen_ready, GEN * p + i + 1)
                if i == 0 and p:
                    act.wait_ge(s_ready, 16 * p)
                if i < 2 * NC:
                    j = 2 * NC * p + i
                    hh, (c0, n) = i // NC, CH[i % NC]
                    if j >= 2:
                        act.wait_ge(q_lo, j - 1)
                        act.wait_ge(q_s, (j - 2 + 1) // NC)
                    hi(qt_[0:NOPE, j % 2, 0:n], ps[0:NOPE, i % 4, 0:n]).then_inc(q_nope, 1)
                    act.wait_ge(q_rope, j + 1)
                    n = min(n, SEQ - c0)
                    hi(qH[0:QK, hh, c0:c0 + n], qt_[0:QK, j % 2, 0:n]).then_inc(q_hi, 1)
                    if c0 + n == SEQ:
                        hi(qs[0:QK, :, 2 * p + hh, :],
                           qt_[0:QK, j % 2, n:n + NS].rearrange("p (b t) -> p b t", b=NB)).then_inc(q_s, 1)
                else:
                    c0 = 512 * (i - 2 * NC)
                    for hh in range(2):
                        hi(kH[0:NOPE, hh, c0:c0 + 512],
                           ps[NOPE * hh:NOPE * hh + NOPE, i % 4, :]).then_inc(gen_hi, 1)

            def move_values(p):
                for j in range(2):
                    act.wait_ge(vg_ready, 2 * p + j + 1)
                    hi(hvH[:, 4 * j:4 * j + 4, :].rearrange("p x n -> p (x n)"), ps[:, 4 + j, :]).then_inc(vg_hi, 1)

            def exponential(u, qi):
                r, qt = 4 * u + qi, 4 * (u % 2) + qi
                n, s = P * (qt + 1), r % 4
                act.wait_ge(s_nm, r + 1)
                if u >= 2 and qi == 0:
                    act.wait_ge(pv_x, tr_count(u - 1))
                nc.scalar.activation(prob[:, prob_at(qt):prob_at(qt) + n],
                                     psf[:, 1024 * (r % 2):1024 * (r % 2) + n], ACT.Exp,
                                     bias=nmx[:, s:s + 1], scale=SCALE,
                                     accum_out=sm[:, s:s + 1]).then_inc(s_exp, 1)

            def move_weighed(u):
                p, hh, blk = u // 4, u // 2 % 2, u % 2
                act.wait_ge(pv_x, tr_count(u + 1))
                part = slice(VH * hh, VH * hh + VH)
                hi(aT[part, p, 512 * blk:512 * blk + 512], ps[part, 6 + u % 2, :]).then_inc(o_free, 1)

            def move_turned(u):
                blk = u % 2
                for kt in range(4 * (blk + 1)):
                    x = tr_count(u) + kt
                    c0 = P * max(0, kt - 4 * blk)
                    act.wait_ge(t_ready, x + 1)
                    if x >= 4:
                        act.wait_ge(pv_x, x - 3)
                    hi(pTH[:, x % 4, c0:512], ps[:, 4 + x % 2, c0:512]).then_inc(t_hi, 1)
                    for i in gens_at(u, kt):
                        move_gen(u // 4 + 1, i)
                    if (qi := row_at(u, kt)) is not None:
                        exponential(u + 1, qi)
                    if kt == 1 and u:
                        move_weighed(u - 1)

            for i in range(GEN):
                move_gen(0, i)
            move_values(0)
            for qi in range(4):
                exponential(0, qi)
            for u in range(UNITS):
                p = u // 4
                move_turned(u)
                if u % 4 == 3 and u < UNITS - 1:
                    move_values(p + 1)
            move_weighed(UNITS - 1)

            act.wait_ge(q4_ready, 1)
            for r in range(KC):
                hi(qlat[:, r, :].rearrange("p (b h t) -> p b h t", b=NB, h=H),
                   ps[:, r, :].rearrange("p (h b t) -> p b h t", b=NB, h=H)).then_inc(q4_e, 1)
            act.wait_ge(q4_ready, 2)
            hi(ctok[:, :], ps[0:NS, 2, 0:KVR]).then_inc(q4_e, 1)

            def sample_exp(b):
                s = b % 2
                act.wait_ge(s4_nm, b + 1)
                if b >= 2:
                    act.wait_ge(t4_ready, b - 1)
                nc.scalar.activation(sp[:, s, :], psf[0:NS, 1536 * s:1536 * s + NEW + NS], ACT.Exp,
                                     bias=nmx[0:NS, s:s + 1], scale=SCALE,
                                     accum_out=sm[0:NS, s:s + 1]).then_inc(s4_exp, 1)

            sample_exp(0)
            for b in range(NB):
                if b + 1 < NB:
                    sample_exp(b + 1)
                act.wait_ge(t4_ready, b + 1)
                if b:
                    act.wait_ge(pv4, b)
                hi(spT[:, 0:PAGES, :].rearrange("p j n -> p (j n)"), ps[:, 6, :]).then_inc(t4_a, 1)
            act.wait_ge(a4, 1)
            hi(aT[:, :, SEQ:T], ps[:, 0, 0:KG * NS].rearrange("p (k n) -> p k n", k=KG)).then_inc(a4_e, 1)

            for k in range(KG):
                hi(mH[:, KG + k, :], gT[:, k, :], g_gmlp[:, k:k + 1]).then_inc(m_hi, 1)

            def squares3(c):
                c0, n = CH[c]
                if c:
                    act.wait_ge(n3_ss, c)
                nc.scalar.activation(sqm[:, :, 0:n], aT[:, :, c0:c0 + n], ACT.Square).then_inc(n3_sq, 1)

            act.wait_ge(a4_e, 1)
            squares3(0)
            for c, (c0, n) in enumerate(CH):
                act.wait_ge(n3_ss, c + 1)
                if c:
                    act.wait_ge(n3_x, c)
                root(rs[:, 0:n], ps[:, 4 + c, 0:n], GW).then_inc(n3_std, 1)
                if c + 1 < NC:
                    squares3(c + 1)
                act.wait_ge(n3_x, c + 1)
                for k in range(KG):
                    hi(mH[:, k, c0:c0 + n], aT[:, k, c0:c0 + n], g_mla[:, k:k + 1]).then_inc(m_hi, 1)

            for m in range(KD):
                act.wait_ge(w_free, NC * (m + 1))
                if m >= 2:
                    act.wait_ge(n4_ss, m - 1)
                nc.scalar.activation(sq2[:, m % 2, :], x2[:, m, :], ACT.Square).then_inc(n4_sq, 1)
            act.wait_ge(n4_ss, KD)
            for c, (c0, n) in enumerate(CH):
                root(rs2[:, c0:c0 + n], ps[:, 4 + c, 0:n], D).then_inc(n4_std, 1)

            def hi4(c):
                c0, n = CH[c]
                for k in range(KD):
                    j = KD * c + k
                    act.wait_ge(h2_x, j + 1)
                    hi(h2H[:, k, c0:c0 + n], htmp[:, j % 4, 0:n]).then_inc(h2_hi, 1)

            for c in range(NC):
                hi4(c)

            def feed_forward(first, i):
                for q in range(2 * NC):
                    s, (c0, n) = q // NC, CH[q % NC]
                    act.wait_ge(gu_ready, 2 * NC * i + (q + 1))
                    if not (first and q < 2):
                        act.wait_ge(f_act, 2 * NC * i + (q - 1))
                    nc.scalar.activation(st[:, q % 2, 0:n], ps[:, 2 * (q % 2), 0:n], ACT.Silu).then_inc(f_silu, 1)
                    act.wait_ge(f_act, 2 * NC * i + (q + 1))
                    if not first:
                        act.wait_ge(dn_ready, NC * KD * i + (KD * (q % NC + 1) - NC * KD))
                    hi(acH[:, s, c0:c0 + n], av[:, q % 2, 0:n]).then_inc(f_hi, 1)

            feed_forward(True, 0)
            with act.Fori(1, NF // 2) as i:
                feed_forward(False, i)

            def squares5(c):
                c0, n = CH[c]
                act.wait_ge(y_free, NC * KD * (NF // 2 - 1) + KD * (c + 1))
                if c:
                    act.wait_ge(n5_ss, c)
                nc.scalar.activation(sq3[:, :, 0:n], x2[:, :, c0:c0 + n], ACT.Square).then_inc(n5_sq, 1)

            squares5(0)
            for c, (c0, n) in enumerate(CH):
                act.wait_ge(n5_ss, c + 1)
                if c:
                    act.wait_ge(n5_x, KD * c)
                root(rs[:, 0:n], ps[:, c, 0:n], D).then_inc(n5_std, 1)
                if c + 1 < NC:
                    squares5(c + 1)

        @block.vector
        def _(dve):
            def scaled(out, x, gain, factor):
                return nc.vector.scalar_tensor_tensor(out, x, gain, factor, ALU.mult, ALU.mult)

            dve.wait_ge(ld_norm1, 16)
            for c, (c0, n) in enumerate(CH):
                dve.wait_ge(n1_std, c + 1)
                nc.vector.reciprocal(rs[:, 0:n], rs[:, 0:n]).then_inc(n1_inv, 1)
                dve.wait_ge(n1_inv, c + 1)
                dve.wait_ge(n1_sq, c + 1)
                for k in range(KD):
                    x = x1[:, k, c0:c0 + n]
                    scaled(x, x, g1[:, k:k + 1], rs[:, 0:n]).then_inc(n1_x, 1)
                for k in range(KD):
                    dve.wait_ge(n1_hi, KD * c + k + 1)
                    nc.vector.tensor_tensor(hL[:, k, c0:c0 + n], x1[:, k, c0:c0 + n], hH[:, k, c0:c0 + n],
                                            ALU.subtract).then_inc(n1_lo, 1)

            dve.wait_ge(ld_const, CONST)
            dve.wait_ge(made, 3)
            for t in range(NT + 1):
                if t < NT:
                    m, slot, s = rows(t), 2 if t == NT - 1 else t % 2, t % 2
                    dve.wait_ge(v_gelu, t + 1)
                    nc.vector.bn_stats(stat6[0:m, s, :], vt[0:m, slot, :]).then_inc(v_b1, 1)
                    dve.wait_ge(v_b1, t + 1)
                    nc.vector.bn_aggr(mv[0:m, s, :], stat6[0:m, s, :]).then_inc(v_b2, 1)
                    dve.wait_ge(v_b2, t + 1)
                    nc.vector.tensor_scalar(ve[0:m, t % 4:t % 4 + 1], mv[0:m, s, 1:2], EPS, None,
                                            ALU.add).then_inc(v_ve, 1)
                if t >= 1:
                    w = t - 1
                    m, slot = rows(w), 2 if w == NT - 1 else w % 2
                    x = vt[0:m, slot, :]
                    dve.wait_ge(v_rv, w + 1)
                    nc.vector.tensor_scalar(x, x, mv[0:m, w % 2, 0:1], rv[0:m, w % 4:w % 4 + 1], ALU.subtract,
                                            ALU.mult).then_inc(v_n1, 1)
                    dve.wait_ge(v_n1, w + 1)
                    nc.vector.tensor_tensor(x, x, vgb[0:m, 0, :], ALU.mult).then_inc(v_n2, 1)
                    dve.wait_ge(v_n2, w + 1)
                    nc.vector.tensor_tensor(x, x, vgb[0:m, 1, :], ALU.add).then_inc(v_fin, 1)
            for g in range(G):
                dve.wait_ge(sp_ready, g + 1)
                nc.vector.tensor_scalar(mix[:, 0:8, GD * g:GD * g + GD],
                                        ps[:, 4 + g % 4, :].rearrange("p (c n) -> p c n", c=8),
                                        bs[:, g:g + 1], None, ALU.add).then_inc(sp_free, 1)
            dve.wait_ge(sp_ready, G + 1)
            grp = "p (g n) -> p g n"
            nc.vector.tensor_tensor(mix[0:NS, 8, :].rearrange(grp, g=G), ps[0:NS, 4, :].rearrange(grp, g=G),
                                    bs8[:, :].unsqueeze(2).broadcast_to((NS, G, GD)), ALU.add).then_inc(sp_free, 1)
            dve.wait_ge(sp_free, G + 1)
            for t in range(NT + 1):
                if t < NT:
                    m = rows(t)
                    dve.wait_ge(u_gelu, t + 1)
                    nc.vector.tensor_tensor(mix[0:m, t, :], vt[0:m, t % 2, :], mix[0:m, t, :],
                                            ALU.mult).then_inc(u_g, 1)
                if t >= 1:
                    w = t - 1
                    m, s = rows(w), slice(w % 4, w % 4 + 1)
                    dve.wait_ge(u_sq, w + 1)
                    nc.vector.tensor_scalar(ve[0:m, s], ssq[0:m, s], 1.0 / GW, EPS, ALU.mult,
                                            ALU.add).then_inc(u_ve, 1)
                    dve.wait_ge(u_rv, w + 1)
                    nc.vector.tensor_scalar(mix[0:m, w, :], mix[0:m, w, :], rv[0:m, s], None,
                                            ALU.mult).then_inc(u_gn, 1)

            def norm2(j):
                c0, n = CH[j % NC]
                k_, x_, g_, out = (KQ, cq, gq, (cqH, cqL)) if j < NC else (KC, ckv, gkv, (ckH, ckL))
                dve.wait_ge(n2_std, j + 1)
                nc.vector.reciprocal(rs[:, 0:n], rs[:, 0:n]).then_inc(n2_inv, 1)
                dve.wait_ge(n2_inv, j + 1)
                for k in range(k_):
                    x = x_[:, k, c0:c0 + n]
                    scaled(x, x, g_[:, k:k + 1], rs[:, 0:n]).then_inc(n2_x, 1)

            def low2(j):
                c0, n = CH[j % NC]
                x, h, lo = (cq, cqH, cqL) if j < NC else (ckv, ckH, ckL)
                dve.wait_ge(n2_hi, j + 1)
                nc.vector.tensor_tensor(lo[:, :, c0:c0 + n], x[:, :, c0:c0 + n], h[:, :, c0:c0 + n],
                                        ALU.subtract).then_inc(n2_lo, 1)

            for j in range(NC):
                norm2(j)
            for j in range(NC):
                low2(j)
            for j in range(NC, 2 * NC):
                norm2(j)
            dve.wait_ge(ld_cs, 16)
            dve.wait_ge(z_ready, NC * (KQ + KC + 1))
            for c, (c0, n) in enumerate(CH):
                b = (NC * (KQ + KC) + c) % 4
                cols = slice(c0, c0 + n)
                nc.vector.tensor_tensor(kr[NOPE:QK, cols], ps[NOPE:QK, b, 0:n], cs[NOPE:QK, cols],
                                        ALU.mult).then_inc(kr_a, 1)
                if c:
                    dve.wait_ge(kr_ok, c)
                nc.vector.tensor_tensor(qr2[NOPE:QK, 0:n], ps[QK:P, b, 0:n], cs[QK:P, cols],
                                        ALU.mult).then_inc(kr_a, 1)
                dve.wait_ge(kr_a, 2 * c + 2)
                nc.vector.tensor_tensor(kr[NOPE:QK, cols], kr[NOPE:QK, cols], qr2[NOPE:QK, 0:n],
                                        ALU.add).then_inc(kr_ok, 1)
            for j in range(NC, 2 * NC):
                low2(j)
            for hh in range(2):
                dve.wait_ge(kr_hi, hh + 1)
                nc.vector.tensor_tensor(kL[NOPE:QK, hh, :], kr[NOPE:QK, 0:SEQ], kH[NOPE:QK, hh, :],
                                        ALU.subtract).then_inc(kr_lo, 1)

            def move_gen(p, i):
                dve.wait_ge(gen_ready, GEN * p + i + 1)
                if i < 2 * NC:
                    j = 2 * NC * p + i
                    c0, n = CH[i % NC]
                    cols = slice(c0, c0 + n)
                    x = qt_[NOPE:QK, j % 2, 0:n]
                    if j >= 2:
                        dve.wait_ge(q_lo, j - 1)
                        dve.wait_ge(q_s, (j - 2 + 1) // NC)
                    nc.vector.tensor_tensor(x, ps[NOPE:QK, i % 4, 0:n], cs[NOPE:QK, cols],
                                            ALU.mult).then_inc(q_cos, 1)
                    dve.wait_ge(q_nope, j + 1)
                    if j:
                        dve.wait_ge(q_rope, j)
                    else:
                        dve.wait_ge(kr_ok, NC)
                    nc.vector.tensor_tensor(qr2[NOPE:QK, 0:n], ps[QK:P, i % 4, 0:n], cs[QK:P, cols],
                                            ALU.mult).then_inc(gen_free, 1)
                    dve.wait_ge(gen_free, GEN * p + i + 1)
                    dve.wait_ge(q_cos, j + 1)
                    nc.vector.tensor_tensor(x, x, qr2[NOPE:QK, 0:n], ALU.add).then_inc(q_rope, 1)
                else:
                    c0 = 512 * (i - 2 * NC)
                    for hh in range(2):
                        dve.wait_ge(gen_hi, 4 * p + 2 * (i - 2 * NC) + hh + 1)
                        ins = nc.vector.tensor_tensor(kL[0:NOPE, hh, c0:c0 + 512],
                                                      ps[NOPE * hh:NOPE * hh + NOPE, i % 4, :],
                                                      kH[0:NOPE, hh, c0:c0 + 512], ALU.subtract)
                    ins.then_inc(gen_free, 1)

            def move_values(p):
                flat = "p x n -> p (x n)"
                for j in range(2):
                    dve.wait_ge(vg_hi, 2 * p + j + 1)
                    nc.vector.tensor_tensor(hvL[:, 4 * j:4 * j + 4, :].rearrange(flat), ps[:, 4 + j, :],
                                            hvH[:, 4 * j:4 * j + 4, :].rearrange(flat),
                                            ALU.subtract).then_inc(vg_free, 1)

            def invert(r):
                s = slice(r % 4, r % 4 + 1)
                dve.wait_ge(s_exp, r + 1)
                u, qi = r // 4, r % 4
                if u and qi < 3:
                    dve.wait_ge(s_pn, 3 * (u - 1) + qi + 1)
                elif u:
                    dve.wait_ge(s_pd, u)
                nc.vector.reciprocal(rsm[:, s], sm[:, s]).then_inc(s_rc, 1)
                if qi == 3:
                    qt = 4 * (u % 2) + 3
                    row = prob[:, prob_at(qt):prob_at(qt + 1)]
                    dve.wait_ge(s_rc, r + 1)
                    nc.vector.tensor_scalar(row, row, rsm[:, s], None, ALU.mult).then_inc(s_pd, 1)

            def maximum(u, qi):
                r, qt = 4 * u + qi, 4 * (u % 2) + qi
                at, s = 1024 * (r % 2), slice(r % 4, r % 4 + 1)
                dve.wait_ge(s_ready, r + 1)
                nc.vector.tensor_reduce(mx[:, s], psf[:, at:at + P * (qt + 1)], AX.X,
                                        ALU.max).then_inc(s_mx, 1)
                dve.wait_ge(s_mx, r + 1)
                nc.vector.tensor_scalar(nmx[:, s], mx[:, s], -SCALE, None, ALU.mult).then_inc(s_nm, 1)

            def move_turned(u):
                blk = u % 2
                for kt in range(4 * (blk + 1)):
                    x = tr_count(u) + kt
                    c0 = P * max(0, kt - 4 * blk)
                    qi = row_at(u, kt)
                    if qi is not None and kt < 4 * blk + 3:
                        maximum(u + 1, qi)
                    if qi:
                        invert(4 * (u + 1) + qi - 1)
                    dve.wait_ge(t_hi, x + 1)
                    nc.vector.tensor_tensor(pTL[:, x % 4, c0:512], ps[:, 4 + x % 2, c0:512],
                                            pTH[:, x % 4, c0:512], ALU.subtract).then_inc(t_free, 1)
                    for i in gens_at(u, kt):
                        move_gen(u // 4 + 1, i)
                    if qi is not None and kt == 4 * blk + 3:
                        maximum(u + 1, qi)
                    if qi == 3:
                        invert(4 * (u + 1) + qi)

            for i in range(GEN):
                move_gen(0, i)
            move_values(0)
            for qi in range(4):
                maximum(0, qi)
                if qi:
                    invert(qi - 1)
            invert(3)
            for u in range(UNITS):
                p = u // 4
                move_turned(u)
                if u % 4 == 3 and u < UNITS - 1:
                    move_values(p + 1)

            def sample_max(b):
                s = b % 2
                new = psf[0:NS, 1536 * s + NEW:1536 * s + NEW + NS]
                dve.wait_ge(s4_ready, b + 1)
                nc.vector.tensor_tensor(new, new, smask[:, b, :], ALU.add).then_inc(s4_mk, 1)
                dve.wait_ge(s4_mk, b + 1)
                nc.vector.tensor_reduce(mx[0:NS, s:s + 1], psf[0:NS, 1536 * s:1536 * s + NEW + NS], AX.X,
                                        ALU.max).then_inc(s4_mx, 1)
                dve.wait_ge(s4_mx, b + 1)
                nc.vector.tensor_scalar(nmx[0:NS, s:s + 1], mx[0:NS, s:s + 1], -SCALE, None,
                                        ALU.mult).then_inc(s4_nm, 1)

            def sample_norm(b):
                s = b % 2
                dve.wait_ge(s4_exp, b + 1)
                nc.vector.reciprocal(rsm[0:NS, s:s + 1], sm[0:NS, s:s + 1]).then_inc(s4_rc, 1)
                dve.wait_ge(s4_rc, b + 1)
                nc.vector.tensor_scalar(sp[:, s, :], sp[:, s, :], rsm[0:NS, s:s + 1], None,
                                        ALU.mult).then_inc(s4_n, 1)

            dve.wait_ge(s_pn, 3 * UNITS)
            dve.wait_ge(s_pd, UNITS)
            sample_max(0)
            sample_norm(0)
            for b in range(NB):
                if b + 1 < NB:
                    sample_max(b + 1)
                dve.wait_ge(t4_ready, b + 1)
                if b:
                    dve.wait_ge(pv4, b)
                nc.vector.tensor_copy(spT[0:NS, PAGES, :],
                                      ps[0:NS, 3 * (b % 2) + 2, NS:2 * NS]).then_inc(t4_b, 1)
                if b + 1 < NB:
                    sample_norm(b + 1)
                dve.wait_ge(pv4, b + 1)
                out = olat[:, :, :].rearrange("p r (h n) -> p r h n", h=H)[:, :, :, TS * b:TS * b + TS]
                nc.vector.tensor_copy(out, ps[:, 7, 0:KC * NS].rearrange("p (r h t) -> p r h t", r=KC,
                                                                       h=H)).then_inc(o4, 1)

            dve.wait_ge(a4, 1)
            for k in range(KG):
                dve.wait_ge(m_hi, k + 1)
                nc.vector.scalar_tensor_tensor(mL[:, KG + k, :], gT[:, k, :], g_gmlp[:, k:k + 1],
                                               mH[:, KG + k, :], ALU.mult, ALU.subtract).then_inc(m_lo, 1)
            for c, (c0, n) in enumerate(CH):
                dve.wait_ge(n3_std, c + 1)
                nc.vector.reciprocal(rs[:, 0:n], rs[:, 0:n]).then_inc(n3_inv, 1)
                dve.wait_ge(n3_inv, c + 1)
                dve.wait_ge(n3_sq, c + 1)
                x = aT[:, :, c0:c0 + n]
                nc.vector.tensor_tensor(x, x, rs[:, 0:n].unsqueeze(1).broadcast_to((P, KG, n)),
                                        ALU.mult).then_inc(n3_x, 1)
                for k in range(KG):
                    dve.wait_ge(m_hi, KG + KG * c + k + 1)
                    nc.vector.scalar_tensor_tensor(mL[:, k, c0:c0 + n], aT[:, k, c0:c0 + n], g_mla[:, k:k + 1],
                                                   mH[:, k, c0:c0 + n], ALU.mult, ALU.subtract).then_inc(m_lo, 1)

            for m in range(KD):
                dve.wait_ge(ld_x2[m // 2], 16)
                for c, (c0, n) in enumerate(CH):
                    q = NC * m + c
                    x = x2[:, m, c0:c0 + n]
                    dve.wait_ge(w_ready, q + 1)
                    nc.vector.tensor_tensor(x, x, ps[:, q % 4, 0:n], ALU.add).then_inc(w_free, 1)
            for c, (c0, n) in enumerate(CH):
                dve.wait_ge(n4_std, c + 1)
                r = rs2[:, c0:c0 + n]
                nc.vector.reciprocal(r, r).then_inc(n4_inv, 1)
                dve.wait_ge(n4_inv, c + 1)
                dve.wait_ge(w_free, NC * KD)
                for k in range(KD):
                    j = KD * c + k
                    if j >= 4:
                        dve.wait_ge(h2_lo, j - 3)
                    scaled(htmp[:, j % 4, 0:n], x2[:, k, c0:c0 + n], g2[:, k:k + 1], r).then_inc(h2_x, 1)

            def feed_forward(first, i):
                for q in range(2 * NC):
                    s, (c0, n) = q // NC, CH[q % NC]
                    a = av[:, q % 2, 0:n]
                    dve.wait_ge(f_silu, 2 * NC * i + (q + 1))
                    if not (first and q < 2):
                        dve.wait_ge(f_lo, 2 * NC * i + (q - 1))
                    nc.vector.tensor_tensor(a, st[:, q % 2, 0:n], ps[:, 2 * (q % 2) + 1, 0:n],
                                            ALU.mult).then_inc(f_act, 1)
                    dve.wait_ge(f_hi, 2 * NC * i + (q + 1))
                    nc.vector.tensor_tensor(acL[:, s, c0:c0 + n], a, acH[:, s, c0:c0 + n],
                                            ALU.subtract).then_inc(f_lo, 1)
                for c, (c0, n) in enumerate(CH):
                    for m in range(KD):
                        r = KD * c + m
                        x = x2[:, m, c0:c0 + n]
                        dve.wait_ge(dn_ready, NC * KD * i + (r + 1))
                        nc.vector.tensor_tensor(x, x, ps[:, 4 + r % 4, 0:n], ALU.add).then_inc(y_free, 1)

            feed_forward(True, 0)
            with dve.Fori(1, NF // 2) as i:
                feed_forward(False, i)
            dve.wait_ge(y_free, NC * KD * (NF // 2))
            for c, (c0, n) in enumerate(CH):
                dve.wait_ge(n5_std, c + 1)
                nc.vector.reciprocal(rs[:, 0:n], rs[:, 0:n]).then_inc(n5_inv, 1)
                dve.wait_ge(n5_inv, c + 1)
                for k in range(KD):
                    x = x2[:, k, c0:c0 + n]
                    scaled(x, x, gf[:, k:k + 1], rs[:, 0:n]).then_inc(n5_x, 1)


def _by_tile(v, k):
    return v.reshape(k, P).T


def _pieces(w, k, step=P):
    m = w.shape[1] // step
    return w.reshape(k, P, m, step).transpose(2, 1, 0, 3).reshape(m, P, k * step)


def kernel(**inputs):
    import numpy as np
    import concourse.bacc as bacc
    from concourse.bass_utils import run_bass_kernel_spmd

    a = {k: np.asarray(v) for k, v in inputs.items()}
    f = np.float32
    x = np.concatenate([a["x_prompt"].reshape(SEQ, D), a["x_sample"].reshape(NS, D)])
    arr = {"x": x.T.reshape(KD, P, T).transpose(1, 0, 2)}
    w_in = a["w_in"][0]
    o_kr = QR + KVR
    o_u = o_kr + ROPE
    o_v = o_u + GW
    half = ROPE // 2
    arr["w_v"] = w_in[:, o_v:].reshape(4, 2, P, GW).transpose(0, 2, 1, 3).reshape(4, P, 1024)
    arr["w_u"] = w_in[:, o_u:o_v].reshape(4, 2, P, GW).transpose(0, 2, 1, 3).reshape(4, P, 1024)
    k_rope = w_in[:, o_kr:o_u]
    k_tile = np.concatenate([np.zeros((D, NOPE), f), k_rope, k_rope[:, half:], k_rope[:, :half]], 1)
    arr["w_in"] = _pieces(np.concatenate([w_in[:, :o_kr], k_tile], 1), KD)
    arr["w_sp"] = a["w_spatial"][0].transpose(2, 0, 1).reshape(P, G * P)
    wbd = np.zeros((NB, TS, G, NB, TS), f)
    for b in range(NB):
        wbd[b, :, :, b, :] = a["w_spatial"][0][:, :TS, :TS].transpose(2, 0, 1)
    arr["wbd"] = wbd.reshape(NS, G, NS)
    arr["bs"] = a["b_spatial"][0].T
    arr["bs8"] = np.tile(a["b_spatial"][0][:, :TS].T, (NB, 1))
    arr["vgb"] = np.broadcast_to(np.stack([a["v_norm_g"][0], a["v_norm_b"][0]]), (P, 2, GW))
    wq = a["w_q_up"][0].reshape(QR, H, QK)
    wq = np.concatenate([wq, wq[:, :, NOPE + half:], wq[:, :, NOPE:NOPE + half]], 2)
    wq = _pieces(wq.reshape(QR, H * P), KQ, 2 * P)
    wk = _pieces(a["w_uk"][0].reshape(KVR, H * NOPE), KC)
    arr["w_qk"] = np.concatenate([wq, wk], 2)
    arr["w_uv"] = _pieces(a["w_uv"][0].reshape(KVR, H * VH), KC)
    arr["w_ukT"] = a["w_uk"][0].transpose(2, 1, 0)
    arr["w_uvr"] = a["w_uv"][0].reshape(KC, P, GW).transpose(1, 0, 2)
    pool = a["cache_ckv"].shape[1]
    rec = np.zeros((pool, P, REC), f)
    ckv = a["cache_ckv"][0]
    rec[:, :, 0:KVR] = ckv.transpose(0, 2, 1).reshape(pool, KC, P, PAGE).transpose(0, 2, 1, 3).reshape(pool, P, KVR)
    rec[:, :, KVR:2 * KVR] = ckv
    arr["cache"] = rec
    arr["cache_r"] = a["cache_krope"][0].transpose(0, 2, 1)
    arr["pages"] = a["page_table"].reshape(1, NB * PAGES)
    arr["w_out"] = _pieces(a["w_out"][0], 2 * KG)
    gate, up = _pieces(a["w_gate"][0], KD), _pieces(a["w_up"][0], KD)
    down = a["w_down"][0].reshape(NF, P, D)
    arr["w_ff"] = np.stack([gate[0::2], up[0::2], gate[1::2], up[1::2], down[0::2], down[1::2]],
                           1).reshape(3 * NF, P, 1024)
    for name, key, k in (("g1", "norm1_g", KD), ("gq", "q_norm_g", KQ), ("gkv", "kv_norm_g", KC),
                         ("g_mla", "out_norm_mla_g", KG), ("g_gmlp", "out_norm_gmlp_g", KG),
                         ("g2", "norm2_g", KD)):
        arr[name] = _by_tile(a[key][0], k)
    arr["gf"] = _by_tile(a["final_norm_g"], KD)
    pos = np.concatenate([np.arange(SEQ), np.tile(NEW + np.arange(TS), NB)]).astype(f)
    inv = (10000.0 ** (-np.arange(half, dtype=f) / half)).astype(f)
    ang = (pos[None, :] * inv[:, None]).astype(f)
    cs = np.zeros((P, T), f)
    cs[NOPE:QK] = np.tile(np.cos(ang), (2, 1))
    cs[QK:P] = np.concatenate([-np.sin(ang), np.sin(ang)])
    arr["cs"] = cs
    arr["ident"] = np.eye(P, dtype=f)
    arr["cmask"] = np.where(np.arange(P)[None, :] <= np.arange(P)[:, None], 0, -1e30).astype(f)
    b_, t_ = np.arange(NS) // TS, np.arange(NS) % TS
    qtok = np.arange(NS) % TS
    see = (b_[None, None, :] == np.arange(NB)[None, :, None]) & (t_[None, None, :] <= qtok[:, None, None])
    arr["smask"] = np.where(see, 0, -1e30).astype(f)

    nc = bacc.Bacc("TRN2", target_bir_lowering=False, num_devices=1)
    dram, sent = {}, {}
    for name, v in arr.items():
        v = np.ascontiguousarray(v)
        sent["in_" + name] = v
        dram[name] = nc.dram_tensor("in_" + name, v.shape, mybir.dt.from_np(v.dtype), kind="ExternalInput").ap()
    for name, shape in (("y", (P, KD, T)), ("ckv_out", (P, KC, T)), ("kr_out", (ROPE, T)), ("v_out", (NS, GW))):
        dram[name] = nc.dram_tensor("out_" + name, shape, F32, kind="ExternalOutput").ap()
    build(nc, dram)
    got = run_bass_kernel_spmd(nc, [sent], core_ids=[0]).results[0]
    y = got["out_y"].transpose(1, 0, 2).reshape(D, T).T
    c = got["out_ckv_out"].transpose(1, 0, 2).reshape(KVR, T).T
    k = got["out_kr_out"].T
    return (y[:SEQ].reshape(1, SEQ, D), y[SEQ:].reshape(NB, TS, D),
            c[:SEQ].reshape(1, 1, SEQ, KVR), k[:SEQ].reshape(1, 1, SEQ, ROPE),
            c[SEQ:].reshape(1, NB, TS, KVR), k[SEQ:].reshape(1, NB, TS, ROPE),
            got["out_v_out"].reshape(1, NB, TS, GW))
```

```python
from contextlib import ExitStack

import concourse.bass as bass
from concourse import mybir

F32 = mybir.dt.float32
F32R = mybir.dt.float32r
I32 = mybir.dt.int32
ALU = mybir.AluOpType
ACT = mybir.ActivationFunctionType
AX = mybir.AxisListType

P = 128
D = 1024
SEQ = 1024
NB, TS = 8, 8
NS = NB * TS
T = SEQ + NS
KD = D // P
H = 8
NOPE, ROPE, VH = 64, 32, 64
QK = NOPE + ROPE
QR, KVR = 384, 256
KQ, KC = QR // P, KVR // P
G, GD = 8, 64
GW = G * GD
KG = GW // P
FF = 2816
NF = FF // P
PAGES, PAGE, POOL = 8, 128, 80
EPS = 1e-6
SCALE = QK ** -0.5
CH = [(0, 384), (384, 384), (768, 320)]
NC = len(CH)
CH1 = [(0, 128), (128, 256), (384, 384), (768, 320)]
J_N1 = 0
J_N2 = J_N1 + len(CH1)
J_N3 = J_N2 + 2 * NC
J_N4 = J_N3 + NC
J_N5 = J_N4 + NC
NT = 9
PAIRS = H // 2
UNITS = 4 * PAIRS
REC = 2 * KVR
CB = 3
NEW = PAGES * PAGE
GEN = 2 * NC + 2

N_V, N_SP, N_U, N_IN = 0, 4, 5, 9
N_HEAD = N_IN + KQ + KC + 1
N_OUT = N_HEAD + 2 * PAIRS
N_FF = N_OUT + KD
MIXED = [*range(KG, 2 * KG), *range(KG)]
U_SPLITS, U_LOWS = (3, 4, 5, 6), (4, 5, 6, 7)
SUM_LAG = 3
BODY = 6


def rows(t):
    return P if t < NT - 1 else NS


def offsets(n):
    return [*range(0, n - P + 1, P)] + ([n - P] if n % P else [])


def tr_count(u):
    return 12 * (u // 2) + 4 * (u % 2)


def gens_at(u, kt):
    return range(2 * kt, 2 * kt + 2) if u % 4 == 3 and u + 1 < UNITS and kt < 4 else ()


def row_at(u, kt):
    qi = kt - (4 if u % 4 == 3 else 0)
    return qi if u + 1 < UNITS and 0 <= qi < 4 else None


def square_at(c, m):
    return 8 + m // (KD - 1) if c % 2 and m in (0, KD - 1) else m


def row_late(u, kt):
    return u % 4 == 3 and kt == 4


def prob_at(qt):
    return P * (qt * (qt + 1) // 2)


def build(nc, d):
    ctx = ExitStack()
    with ctx:
        class Region:
            def __init__(self, start, end=None):
                self.start, self.here, self.end = start, start, end

            def put(self, name, shape, dt=F32):
                n = 4
                for s in shape[1:]:
                    n *= s
                t = nc.alloc_sbuf_tensor_at(name, shape, dt, offset=self.here)
                self.here += (n + 31) // 32 * 32
                assert self.end is None or self.here <= self.end, name
                return t

        small = Region((nc.sbuf_base + 63) // 64 * 64)
        ident = small.put("ident", [P, P])
        ones = small.put("ones", [P, P])
        cmask, cmaskR = small.put("cmask", [P, P]), small.put("cmaskR", [P, P], F32R)
        identR = small.put("identR", [P, P], F32R)
        mask0 = small.here
        smask = small.put("smask", [NS, NB, NS])
        qr2 = Region(mask0, small.here).put("qr2", [P, 384])
        diag = small.put("diag", [P, 3, P])
        rope0 = small.here
        cs = small.put("cs", [P, T])
        vgb = Region(rope0).put("vgb", [P, 2, GW])
        g1, gq, gkv = small.put("g1", [P, KD]), small.put("gq", [P, KQ]), small.put("gkv", [P, KC])
        g_mla, g_gmlp = small.put("g_mla", [P, KG]), small.put("g_gmlp", [P, KG])
        g2, gf = small.put("g2", [P, KD]), small.put("gf", [P, KD])
        bs, bs8 = small.put("bs", [P, G]), small.put("bs8", [NS, G])
        pages = small.put("pages", [1, NB * PAGES], I32)
        mhalf = small.put("mhalf", [P, 1])
        stat6, mv = small.put("stat6", [P, 2, 6]), small.put("mv", [P, 2, 2])
        sums = small.put("sums", [P, 3])
        ms, rt = small.put("ms", [P, 4, 3]), small.put("rt", [P, 4, 3])
        ve, rv, ssq = (small.put(n, [P, 4]) for n in ("ve", "rv", "ssq"))
        mx, nmx, sm, rsm = (small.put(n, [P, 4]) for n in ("mx", "nmx", "sm", "rsm"))

        A0 = (small.here + 63) // 64 * 64
        B0 = A0 + 8 * T * KD + 1024
        C0 = B0 + 8 * T * KD
        W0 = C0 + 4 * T * KD + 1024
        R0 = W0 + 4 * 4096
        assert R0 + 2 * 4096 <= nc.sbuf_usable_end, (R0 + 8192, nc.sbuf_usable_end)

        raw = Region(R0).put("raw", [P, 2, 1024])
        reg = Region(W0, R0)
        wH, wL = [None, None], [None, None]
        for s in range(2):
            wH[s], wL[s] = reg.put(f"w{s}H", [P, 1024], F32R), reg.put(f"w{s}L", [P, 1024], F32R)

        reg = Region(W0, R0)
        spH, spL = reg.put("spH", [P, G, P], F32R), reg.put("spL", [P, G, P], F32R)
        ut = reg.put("ut", [P, 2, GW])
        vs = reg.put("vs", [P, GW])
        wbd = reg.put("wbd", [NS, G, NS])
        reg = Region(A0, B0)
        hH, hL = reg.put("hH", [P, KD, T], F32R), reg.put("hL", [P, KD, T], F32R)
        reg = Region(B0, C0)
        vwH, vwL = reg.put("vwH", [P, KD, GW], F32R), reg.put("vwL", [P, KD, GW], F32R)
        sq0 = Region(C0 - 4 * KD * 384, C0).put("sq0", [P, KD, 384])
        vH = reg.put("vH", [P, NT, GW], F32R)
        v0 = reg.here
        vL = reg.put("vL", [P, NT, GW], F32R)
        vf = Region(v0, C0).put("vf", [P, NT, GW])
        mix = Region(B0).put("mix", [P, NT, GW])
        gT = Region(C0 - 4 * KG * T, C0).put("gT", [P, KG, T])
        x1 = Region(C0, W0).put("x1", [P, KD, T])
        reg = Region(C0, W0)
        uwH, uwL = reg.put("uwH", [P, KD, GW], F32R), reg.put("uwL", [P, KD, GW], F32R)

        reg = Region(B0, C0 - 4 * KG * T)
        cqH, cqL = reg.put("cqH", [P, KQ, T], F32R), reg.put("cqL", [P, KQ, T], F32R)
        PT0 = reg.here
        cq = Region(PT0).put("cq", [P, KQ, T])
        pTH, pTL = reg.put("pTH", [P, 4, 512], F32R), reg.put("pTL", [P, 4, 512], F32R)
        PT1 = reg.here
        ckv = reg.put("ckv", [P, KC, T])
        uvH = reg.put("uvH", [P, KC, P], F32R)
        reg = Region(C0, W0)
        sq1 = Region(C0).put("sq1", [P, 3, KQ, 384])
        aT = reg.put("aT", [P, KG, T])
        ckH, ckL = reg.put("ckH", [P, KC, T], F32R), reg.put("ckL", [P, KC, T], F32R)
        uvL = reg.put("uvL", [P, KC, P], F32R)
        reg = Region(A0, B0)
        kH, kL = reg.put("kH", [P, 2, SEQ], F32R), reg.put("kL", [P, 2, SEQ], F32R)
        qH, qL = reg.put("qH", [P, 2, SEQ], F32R), reg.put("qL", [P, 2, SEQ], F32R)
        hvH, hvL = reg.put("hvH", [P, 8, P], F32R), reg.put("hvL", [P, 8, P], F32R)
        prob = reg.put("prob", [P, prob_at(8)])
        KR0 = reg.here
        kr = reg.put("kr", [P, T])
        qt_ = reg.put("qt", [P, 3, 384])
        qs = reg.put("qs", [P, NB, H, TS])

        reg = Region(A0, KR0)
        cp1, cp2 = reg.put("cp1", [P, PAGES, REC]), reg.put("cp2", [P, PAGES, REC])
        assert reg.here == A0 + 4 * 8 * SEQ
        cpr = Region(C0 + 4 * KG * T, W0).put("cpr", [P, CB, PAGES, PAGE])
        sp = reg.put("sprob", [NS, 2, NEW + NS])
        reg = Region(B0, PT0)
        olat = reg.put("olat", [P, KC, 512])
        cp = [reg.put("cp0", [P, PAGES, REC]), cp1, cp2]
        qlat, ctok = reg.put("qlat", [P, KC, 512]), reg.put("ctok", [NS, KVR])
        reg = Region(PT0, PT1)
        uvr = reg.put("uvr", [P, KC, GW])
        spT = reg.put("spT", [P, PAGES + 1, NS])
        sqm = reg.put("sqm", [P, KG, 384])
        ukT = Region(R0).put("ukT", [NOPE, H, KVR])

        reg = Region(A0, B0)
        mH, mL = reg.put("mH", [P, 2 * KG, T], F32R), reg.put("mL", [P, 2 * KG, T], F32R)
        sq2 = Region(B0).put("sq2", [P, 3, T])
        x2 = Region(C0, W0).put("x2", [P, KD, T])
        reg = Region(B0, C0)
        h2H, h2L = reg.put("h2H", [P, KD, T], F32R), reg.put("h2L", [P, KD, T], F32R)
        sq3 = Region(B0).put("sq3", [P, 10, 384])
        reg = Region(A0, B0)
        upH, upL, dnH, dnL = ([reg.put(f"{n}{s}", [P, 1024], F32R) for s in range(2)]
                              for n in ("upH", "upL", "dnH", "dnL"))
        acH, acL = reg.put("acH", [P, 2, T], F32R), reg.put("acL", [P, 2, T], F32R)
        st, av = reg.put("st", [P, 2, 384]), reg.put("av", [P, 2, 384])
        htmp = reg.put("htmp", [P, 4, 384])
        picked = reg.put("picked", [P, 3, P])

        ps = ctx.enter_context(nc.psum_tensor("ps", [P, 8, 512], F32))
        psf = ps[:, :, :].rearrange("p b n -> p (b n)")

        def v_tile(t):
            return vf[:, t, :] if t < NT - 1 else vs[0:NS, :]

        def sem(name):
            return ctx.enter_context(nc.semaphore(name))

        ld_norm1, ld_const, ld_cs, ld_uk, ld_uv = (
            sem(n) for n in ("ld_norm1", "ld_const", "ld_cs", "ld_uk", "ld_uv"))
        ld_x = [sem(f"ld_x{c}") for c in range(len(CH1))]
        ld_x2 = [sem(f"ld_x2_{j}") for j in range(4)]
        raw_full = [sem(f"raw_full{s}") for s in range(2)]
        cp_full = [sem(f"cp_full{s}") for s in range(CB)]
        out_v, out_ckv, out_kr, out_y = sem("out_v"), sem("out_ckv"), sem("out_kr"), sem("out_y")
        made, made_r, sp_masked, split_seen, split_hi, split_lo = (
            sem(n) for n in ("made", "made_r", "sp_masked", "split_seen", "split_hi", "split_lo"))
        nm_sq, nm_sum, nm_pick, nm_column, nm_mean, nm_pow, nm_diag, nm_spread = (
            sem("nm_" + n) for n in ("sq", "sum", "pick", "column", "mean", "pow", "diag", "spread"))
        n1_x, n1_hi, n1_lo = (sem("n1_" + n) for n in ("x", "hi", "lo"))
        v_ready, v_gelu, v_b1, v_b2, v_ve, v_rv, v_n1, v_n2, v_fin, v_hi, v_lo = (
            sem("v_" + n) for n in ("ready", "gelu", "b1", "b2", "ve", "rv", "n1", "n2", "fin", "hi", "lo"))
        sp_ready, sp_free = sem("sp_ready"), sem("sp_free")
        u_ready, u_gelu, u_g, u_sq, u_ve, u_rv, u_gn, u_tr, u_out = (
            sem("u_" + n) for n in ("ready", "gelu", "g", "sq", "ve", "rv", "gn", "tr", "out"))
        z_ready, z_free = sem("z_ready"), sem("z_free")
        kr_a, kr_ok, kr_hi, kr_lo = sem("kr_a"), sem("kr_ok"), sem("kr_hi"), sem("kr_lo")
        n2_x, n2_hi, n2_lo = (sem("n2_" + n) for n in ("x", "hi", "lo"))
        gen_ready, gen_free, gen_hi = sem("gen_ready"), sem("gen_free"), sem("gen_hi")
        q_nope, q_cos, q_rope, q_hi, q_lo, q_s = (
            sem("q_" + n) for n in ("nope", "cos", "rope", "hi", "lo", "s"))
        vg_ready, vg_hi, vg_free = sem("vg_ready"), sem("vg_hi"), sem("vg_free")
        s_ready, s_mx, s_nm, s_exp, s_rc, s_pn, s_pd = (
            sem("s_" + n) for n in ("ready", "mx", "nm", "exp", "rc", "pn", "pd"))
        t_ready, t_hi, t_free, pv_x, o_free = (sem(n) for n in ("t_ready", "t_hi", "t_free", "pv_x", "o_free"))
        q4_ready, q4_e = sem("q4_ready"), sem("q4_e")
        s4_ready, s4_mk, s4_mx, s4_nm, s4_exp, s4_rc, s4_n = (
            sem("s4_" + n) for n in ("ready", "mk", "mx", "nm", "exp", "rc", "n"))
        t4_ready, t4_a, t4_b, pv4, o4, a4, a4_e = (
            sem(n) for n in ("t4_ready", "t4_a", "t4_b", "pv4", "o4", "a4", "a4_e"))
        n3_x = sem("n3_x")
        m_hi, m_lo, w_ready, w_free = sem("m_hi"), sem("m_lo"), sem("w_ready"), sem("w_free")
        n4_sq, n4_added = sem("n4_sq"), sem("n4_added")
        h2_x, h2_hi, h2_lo = sem("h2_x"), sem("h2_hi"), sem("h2_lo")
        gu_ready, f_silu, f_act, f_hi, f_lo, dn_ready, y_free = (
            sem(n) for n in ("gu_ready", "f_silu", "f_act", "f_hi", "f_lo", "dn_ready", "y_free"))
        n5_sq, n5_add, n5_x = sem("n5_sq"), sem("n5_add"), sem("n5_x")

        const_loads = [(vgb, "vgb"), (wbd, "wbd"), (bs, "bs"), (bs8, "bs8"),
                       (gq, "gq"), (gkv, "gkv"), (cmask, "cmask"), (smask, "smask"),
                       (g_mla, "g_mla"), (g_gmlp, "g_gmlp"), (g2, "g2"), (gf, "gf"), (pages, "pages")]
        CONST = 16 * len(const_loads)

        def gw(t, j):
            return t[:, 2 * j:2 * j + 2, :].rearrange("p k n -> p (k n)")

        block = ctx.enter_context(nc.Block())

        @block.sync
        def _(sp_):
            def piece(n, src, width=1024):
                if n >= 2:
                    sp_.wait_ge(split_lo, n - 1)
                sp_.dma_start(raw[:, n % 2, 0:width], src).then_inc(raw_full[n % 2], 16)

            def load_x(c):
                c0, n = CH1[c]
                sp_.dma_start(x1[:, :, c0:c0 + n], d["x"][:, :, c0:c0 + n]).then_inc(ld_x[c], 16)

            load_x(0)
            for t, name in ((ident, "ident"), (g1, "g1")):
                sp_.dma_start(t[:, :], d[name]).then_inc(ld_norm1, 16)
            piece(N_V, d["w_v"][0])
            piece(N_V + 1, d["w_v"][1])
            load_x(1)
            piece(N_V + 2, d["w_v"][2])
            piece(N_V + 3, d["w_v"][3])
            load_x(2)
            for t, name in const_loads:
                full = tuple(slice(None) for _ in t.shape)
                sp_.dma_start(t[full], d[name]).then_inc(ld_const, 16)
            load_x(3)
            piece(N_SP, d["w_sp"])
            for j in range(4):
                piece(N_U + j, d["w_u"][j])
            sp_.wait_ge(v_fin, NT)
            sp_.dma_start(d["v_out"], vs[0:NS, :]).then_inc(out_v, 16)
            sp_.dma_start(cs[:, :], d["cs"]).then_inc(ld_cs, 16)
            for m in range(KQ + KC + 1):
                piece(N_IN + m, d["w_in"][m])
            for p in range(PAIRS):
                piece(N_HEAD + 2 * p, d["w_qk"][p])
                piece(N_HEAD + 2 * p + 1, d["w_uv"][p], KC * P)
                if p == 0:
                    sp_.wait_ge(n2_x, KQ * NC + KC * NC)
                    sp_.dma_start(d["ckv_out"], ckv[:, :, :]).then_inc(out_ckv, 16)
                    sp_.wait_ge(kr_ok, NC)
                    sp_.dma_start(d["kr_out"], kr[NOPE:QK, :]).then_inc(out_kr, 16)
            for m in range(2):
                piece(N_OUT + m, d["w_out"][m])

            def page_numbers(b):
                return [sp_.value_load(pages[0:1, b * PAGES + j:b * PAGES + j + 1], min_val=0,
                                       max_val=POOL - 1) for j in range(PAGES)]

            def fetch(b, numbers, latents=True, ropes=True):
                for j, page in enumerate(numbers):
                    if latents:
                        src = d["cache"][bass.ds(page, 1), :, :].rearrange("a p n -> (a p) n")
                        sp_.dma_start(cp[b % CB][:, j, :], src).then_inc(cp_full[b % CB], 16)
                    if ropes:
                        src = d["cache_r"][bass.ds(page, 1), :, :].rearrange("a p n -> (a p) n")
                        sp_.dma_start(cpr[NOPE:QK, b % CB, j, :], src).then_inc(cp_full[b % CB], 16)

            sp_.wait_ge(gen_ready, GEN * PAIRS)
            sp_.wait_ge(ld_const, CONST)
            fetch(0, page_numbers(0), ropes=False)
            sp_.wait_ge(split_lo, N_OUT + 2)
            sp_.dma_start(ukT[:, :, :], d["w_ukT"]).then_inc(ld_uk, 16)
            sp_.wait_ge(vg_ready, 2 * PAIRS)
            fetch(0, page_numbers(0), latents=False)
            sp_.wait_ge(s_ready, 4 * UNITS)
            for b in range(1, CB):
                fetch(b, page_numbers(b))
            sp_.wait_ge(pv_x, tr_count(UNITS))
            sp_.dma_start(uvr[:, :, :], d["w_uvr"]).then_inc(ld_uv, 16)
            for b in range(CB, NB):
                numbers = page_numbers(b)
                sp_.wait_ge(pv4, b - CB + 1)
                fetch(b, numbers)
            sp_.wait_ge(m_lo, 2 * KG * NC)
            for m in range(2, KD):
                if m < 6:
                    j = m - 2
                    sp_.dma_start(x2[:, 2 * j:2 * j + 2, :], d["x"][:, 2 * j:2 * j + 2, :]).then_inc(ld_x2[j], 16)
                piece(N_OUT + m, d["w_out"][m])
            with sp_.Fori(0, NF // 2) as i:
                for j in range(BODY):
                    n = N_FF + j
                    sp_.wait_ge(split_lo, BODY * i + (n - 1))
                    src = d["w_ff"][bass.ds(BODY * i + j, 1), :, :].rearrange("a p n -> (a p) n")
                    sp_.dma_start(raw[:, n % 2, :], src).then_inc(raw_full[n % 2], 16)
            for c, (c0, n) in enumerate(CH):
                for k in (0, KD // 2):
                    half = slice(k, k + KD // 2)
                    sp_.wait_ge(n5_x, KD * c + k + KD // 2)
                    sp_.dma_start(d["y"][:, half, c0:c0 + n], x2[:, half, c0:c0 + n]).then_inc(out_y, 16)
            sp_.wait_ge(out_v, 16)
            sp_.wait_ge(out_ckv, 16)
            sp_.wait_ge(out_kr, 16)
            sp_.wait_ge(out_y, 2 * 16 * NC)

        @block.gpsimd
        def _(pool):
            def split(n, hi, lo, width=1024, turns=0, i=0):
                r = raw[:, n % 2, 0:width]
                pool.wait_ge(raw_full[n % 2], 16 * (n // 2 + 1) + 8 * turns * i)
                if turns:
                    pool.sem_inc(split_seen, 1)
                pool.tensor_scalar(hi, r, 1.0, 0.0, ALU.mult, ALU.add).then_inc(split_hi, 1)
                if lo is not None:
                    pool.wait_ge(split_hi, n + 1 + turns * i)
                    pool.tensor_tensor(lo, r, hi, ALU.subtract).then_inc(split_lo, 1)

            def power(j):
                pool.wait_ge(nm_mean, j + 1)
                pool.tensor_tensor(rt[:, j % 4, :], ms[:, j % 4, :], mhalf[:, :].broadcast_to((P, 3)),
                                   ALU.pow).then_inc(nm_pow, 1)

            def add_squares(m):
                pool.wait_ge(n4_sq, m + 1)
                if m >= 2:
                    pool.wait_ge(n4_added, m - 1)
                pool.tensor_tensor(sq2[:, 0, :], sq2[:, 0, :], sq2[:, 1 + m % 2, :],
                                   ALU.add).then_inc(n4_added, 1)

            pool.memset(ones[:, :], 1.0).then_inc(made, 1)
            pool.memset(mhalf[:, :], -0.5).then_inc(made, 1)
            pool.memset(ms[:, :, :], 1.0).then_inc(made, 1)
            pool.wait_ge(made, 3)
            for j in range(4):
                split(N_V + j, gw(vwH, j), None)
                if j == 0:
                    power(J_N1)
            power(J_N1 + 1)
            power(J_N1 + 2)
            def spatial_weights():
                pool.wait_ge(raw_full[N_SP % 2], 16 * (N_SP // 2 + 1))
                rsp = raw[:, N_SP % 2, :].rearrange("p (g i) -> p g i", g=G)
                pool.affine_select(out=rsp, in_=rsp, compare_op=ALU.is_ge, fill=0.0, base=0,
                                   pattern=[[0, G], [1, P]], channel_multiplier=-1).then_inc(sp_masked, 1)
                pool.wait_ge(ld_const, CONST)
                pool.affine_select(out=wbd[:, :, :], in_=wbd[:, :, :], compare_op=ALU.is_ge, fill=0.0, base=0,
                                   pattern=[[0, G], [1, NS]], channel_multiplier=-1).then_inc(sp_masked, 1)
                pool.wait_ge(sp_masked, 2)
                flat = "p g i -> p (g i)"
                split(N_SP, spH[:, :, :].rearrange(flat), spL[:, :, :].rearrange(flat))

            for t in range(NT + 1):
                if t < NT:
                    m, s = rows(t), t % 4
                    pool.wait_ge(v_ve, t + 1)
                    pool.tensor_tensor(rv[0:m, s:s + 1], ve[0:m, s:s + 1], mhalf[0:m, :],
                                       ALU.pow).then_inc(v_rv, 1)
                if t == 1:
                    power(J_N1 + 3)
                if t >= 2:
                    w = t - 2
                    pool.wait_ge(v_hi, w + 1)
                    pool.tensor_tensor(vL[:, w, :], vf[:, w, :], vH[:, w, :], ALU.subtract).then_inc(v_lo, 1)
                if t == 2:
                    spatial_weights()
                elif t in U_SPLITS:
                    pool.wait_ge(n1_lo, KD * len(CH1))
                    j = U_SPLITS.index(t)
                    split(N_U + j, gw(uwH, j), None)

            def in_piece(m):
                split(N_IN + m, wH[m % 2][:, :], wL[m % 2][:, :])

            for t in range(NT):
                m, s = rows(t), t % 4
                pool.wait_ge(u_ve, t + 1)
                pool.tensor_tensor(rv[0:m, s:s + 1], ve[0:m, s:s + 1], mhalf[0:m, :], ALU.pow).then_inc(u_rv, 1)
                if t == 2:
                    pool.wait_ge(sp_ready, G + 1)
                    in_piece(0)
            pool.wait_ge(u_sq, NT)
            pool.wait_ge(u_g, NT)
            pool.wait_ge(out_v, 16)
            in_piece(1)
            for m in range(2, KQ + KC + 1):
                pool.wait_ge(z_ready, NC * (m - 1))
                in_piece(m)
                if m >= KQ + KC - 1:
                    for j in range(NC):
                        power(J_N2 + NC * (m - KQ - KC + 1) + j)

            def head_pieces(p):
                if p < 2:
                    pool.wait_ge(z_ready, NC * (KQ + KC + 1 if p else KQ + KC))
                else:
                    pool.wait_ge(gen_ready, GEN * (p - 1))
                split(N_HEAD + 2 * p, wH[p % 2][:, :], wL[p % 2][:, :])
                if p:
                    pool.wait_ge(vg_ready, 2 * p)
                flat = "p k n -> p (k n)"
                split(N_HEAD + 2 * p + 1, uvH[:, :, :].rearrange(flat), uvL[:, :, :].rearrange(flat), KC * P)

            def query_lo(p):
                for hh in range(2):
                    for c, (c0, n) in enumerate(CH):
                        j = 2 * NC * p + NC * hh + c
                        n = min(n, SEQ - c0)
                        pool.wait_ge(q_hi, j + 1)
                        pool.tensor_tensor(qL[0:QK, hh, c0:c0 + n], qt_[0:QK, j % 3, 0:n],
                                           qH[0:QK, hh, c0:c0 + n], ALU.subtract).then_inc(q_lo, 1)

            def normalise(u):
                for qi in range(3):
                    r, qt = 4 * u + qi, 4 * (u % 2) + qi
                    n = P * (qt + 1)
                    row = prob[:, prob_at(qt):prob_at(qt) + n]
                    pool.wait_ge(s_rc, r + 1)
                    pool.tensor_tensor(row, row, rsm[:, r % 4:r % 4 + 1].broadcast_to((P, n)),
                                       ALU.mult).then_inc(s_pn, 1)

            head_pieces(0)
            pool.wait_ge(split_lo, N_HEAD + 2)
            pool.wait_ge(kr_hi, 2)
            pool.tensor_tensor(kL[NOPE:QK, 1, :], kr[NOPE:QK, 0:SEQ], kH[NOPE:QK, 1, :],
                               ALU.subtract).then_inc(kr_lo, 1)
            pool.wait_ge(kr_lo, 2)
            query_lo(0)
            head_pieces(1)
            normalise(0)
            for u in range(UNITS):
                p = u // 4
                if u % 4 == 3 and u < UNITS - 1:
                    query_lo(p + 1)
                if u < UNITS - 1:
                    normalise(u + 1)
                if u % 4 == 3 and p + 2 < PAIRS:
                    head_pieces(p + 2)
                if UNITS - 4 <= u < UNITS - 2:
                    pool.wait_ge(gen_ready, GEN * PAIRS)
                    m = u - (UNITS - 4)
                    split(N_OUT + m, wH[m % 2][:, :], wL[m % 2][:, :])
            for j in range(NC):
                power(J_N3 + j)
            for m in range(2, KD):
                pool.wait_ge(w_ready, NC * (m - 1))
                split(N_OUT + m, wH[m % 2][:, :], wL[m % 2][:, :])
                if m >= 3:
                    add_squares(m - 2)
            add_squares(KD - 2)

            def ff_pieces(first, i, after_h2):
                for s in range(2):
                    if first and s == 0:
                        pool.wait_ge(w_ready, NC * (KD - 1))
                    elif not first:
                        pool.wait_ge(gu_ready, 2 * NC * i + (NC * (s - 1)))
                    n = N_FF + 2 * s
                    if not (first and s):
                        split(n, wH[s][:, :], wL[s][:, :], turns=BODY, i=i)
                    if first and s == 0:
                        power(J_N4)
                        power(J_N4 + 1)
                        pool.wait_ge(w_ready, NC * KD)
                    split(n + 1, upH[s][:, :], upL[s][:, :], turns=BODY, i=i)
                    if first and s == 0:
                        after_h2()
                if not first:
                    pool.wait_ge(dn_ready, NC * KD * i)
                for s in range(2):
                    split(N_FF + 4 + s, dnH[s][:, :], dnL[s][:, :], turns=BODY, i=i)

            def h2_lows():
                power(J_N4 + 2)
                for c, (c0, n) in list(enumerate(CH))[1:]:
                    if c == 2:
                        split(N_FF + 2, wH[1][:, :], wL[1][:, :], turns=BODY)
                    for k in range(KD):
                        j = KD * c + k
                        pool.wait_ge(h2_hi, j + 1)
                        pool.tensor_tensor(h2L[:, k, c0:c0 + n], htmp[:, j % 4, 0:n], h2H[:, k, c0:c0 + n],
                                           ALU.subtract).then_inc(h2_lo, 1)

            ff_pieces(True, 0, h2_lows)
            with pool.Fori(1, NF // 2) as i:
                ff_pieces(False, i, None)
            for c, (c0, n) in enumerate(CH):
                for m in range(1, KD - 1):
                    r = (KD - 2) * c + m - 1
                    total = sq3[:, square_at(c, 0), 0:n]
                    pool.wait_ge(n5_sq, KD * c + m + 1)
                    if r:
                        pool.wait_ge(n5_add, r)
                    pool.tensor_tensor(total, total, sq3[:, square_at(c, m), 0:n], ALU.add).then_inc(n5_add, 1)
                    if c and m == SUM_LAG:
                        power(J_N5 + c - 1)
            power(J_N5 + NC - 1)

        @block.tensor
        def _(pe):
            def mm3(out, wh, wl, xh, xl, start, stop):
                nc.tensor.matmul(out, wh, xh, start=start, stop=False)
                nc.tensor.matmul(out, wh, xl, start=False, stop=False)
                return nc.tensor.matmul(out, wl, xh, start=False, stop=stop)

            def sum_squares(j, bank, sq, k, n):
                pe.wait_ge(nm_sq, j + 1)
                for kk in range(k):
                    last = nc.tensor.matmul(ps[:, bank, 0:n], ones[:, :], sq[:, kk, 0:n], start=kk == 0,
                                            stop=kk == k - 1)
                last.then_inc(nm_sum, 1)

            def spread(j, bank, n):
                pe.wait_ge(nm_diag, j + 1)
                for i, o in enumerate(offsets(n)):
                    last = nc.tensor.matmul(ps[:, bank, o:o + P], ones[:, :], diag[:, i, :],
                                            start=True, stop=True)
                last.then_inc(nm_spread, 1)

            pe.wait_ge(made, 1)

            def sum1(c):
                sum_squares(J_N1 + c, 4 + c, sq0, KD, CH1[c][1])

            def spread1(c):
                spread(J_N1 + c, 4 + c, CH1[c][1])

            sum1(0)
            spread1(0)
            for t in range(NT):
                m, b = rows(t), t % 4
                if t == 2:
                    spread1(2)
                    sum1(3)
                elif t == 4:
                    spread1(3)
                if t >= 4:
                    pe.wait_ge(v_gelu, t - 3)
                cols = slice(P * t, P * t + m)
                for k in range(KD):
                    if t == 0 and k % 2 == 0:
                        pe.wait_ge(split_lo, N_V + k // 2 + 1)
                    if t == 0 and k == KD // 2:
                        sum1(1)
                    if (c := {0: 0, 1: 1, 3: 2, 6: 3}.get(t)) is not None:
                        pe.wait_ge(n1_lo, KD * c + k + 1)
                    last = mm3(ps[0:m, b, :], hH[:, k, cols], hL[:, k, cols], vwH[:, k, :], vwL[:, k, :],
                               k == 0, k == KD - 1)
                last.then_inc(v_ready, 1)
                if t == 0:
                    spread1(1)
                    sum1(2)
            def spatial():
                pe.wait_ge(split_lo, N_U)
                pe.wait_ge(v_lo, NT - 1)
                for g in range(G):
                    b = 4 + g % 4
                    if g >= 4:
                        pe.wait_ge(sp_free, g - 3)
                    else:
                        pe.wait_ge(n1_x, KD * len(CH1))
                    out = ps[:, b, :].rearrange("p (c n) -> p c n", c=8)
                    cols = slice(GD * g, GD * g + GD)
                    mm3(out, spH[:, g, :], spL[:, g, :], vH[:, 0:8, cols], vL[:, 0:8, cols],
                        True, True).then_inc(sp_ready, 1)
                pe.wait_ge(v_fin, NT)
                pe.wait_ge(sp_masked, 2)
                pe.wait_ge(sp_free, 5)
                for g in range(G):
                    last = nc.tensor.matmul(ps[0:NS, 4, GD * g:GD * g + GD], wbd[:, g, :],
                                            vs[0:NS, GD * g:GD * g + GD], start=True, stop=True)
                last.then_inc(sp_ready, 1)

            for t in range(NT + 2):
                if t < NT:
                    m, b = rows(t), (t + 1) % 4
                    if t >= 4:
                        pe.wait_ge(u_gelu, t - 3)
                    else:
                        pe.wait_ge(v_gelu, NT - 3 + t)
                    cols = slice(P * t, P * t + m)
                    for k in range(KD):
                        if t == 0 and k % 2 == 0:
                            pe.wait_ge(split_lo, N_U + k // 2 + 1)
                        last = mm3(ps[0:m, b, :], hH[:, k, cols], hL[:, k, cols], uwH[:, k, :], uwL[:, k, :],
                                   k == 0, k == KD - 1)
                    last.then_inc(u_ready, 1)
                if t == 1:
                    spatial()
                if t >= 2:
                    w = t - 2
                    m, b = rows(w), 5 + w % 2
                    pe.wait_ge(u_gn, w + 1)
                    if w >= 2:
                        pe.wait_ge(u_out, w - 1)
                    else:
                        pe.wait_ge(sp_free, G + 1)
                    for j in range(KG):
                        last = nc.tensor.transpose(ps[:, b, P * j:P * j + m], mix[0:m, w, P * j:P * j + P],
                                                   ident[0:m, 0:m])
                    last.then_inc(u_tr, 1)
            pe.wait_ge(u_gelu, NT)
            sums = {9: (0,), 10: (1,), 11: (2,), 15: (3, 4), 16: (5,)}
            spreads = {10: (0,), 11: (1,), 12: (2,), 16: (3, 4), 17: (5,)}
            for m in range(KQ + KC + 1):
                pe.wait_ge(split_lo, N_IN + m + 1)
                s = m % 2
                for c, (c0, n) in enumerate(CH):
                    q = NC * m + c
                    if q >= 4:
                        pe.wait_ge(z_free, q - 3)
                    for k in range(KD):
                        w = slice(P * k, P * k + P)
                        last = mm3(ps[:, q % 4, 0:n], wH[s][:, w], wL[s][:, w], hH[:, k, c0:c0 + n],
                                   hL[:, k, c0:c0 + n], k == 0, k == KD - 1)
                    last.then_inc(z_ready, 1)
                    for j in spreads.get(q, ()):
                        spread(J_N2 + j, 4 + j % NC, CH[j % NC][1])
                    for j in sums.get(q, ()):
                        if j == 0:
                            pe.wait_ge(u_out, NT)
                        elif j >= NC:
                            pe.wait_ge(n2_x, KQ * (j - NC + 1))
                        sum_squares(J_N2 + j, 4 + j % NC, sq1[:, j % 3, :, :], KQ if j < NC else KC,
                                    CH[j % NC][1])

            def query_key(p, i):
                s = p % 2
                if i == 0:
                    pe.wait_ge(split_lo, N_HEAD + 2 * p + 1)
                    if p == 0:
                        pe.wait_ge(n2_lo, 2 * NC)
                        pe.wait_ge(z_free, NC * (KQ + KC))
                        pe.wait_ge(kr_ok, 2)
                if p == 0 and i == 1:
                    pe.wait_ge(kr_ok, NC)
                if p and i in (0, 2):
                    pe.wait_ge(s_exp, 16 * p - 1 + i // 2)
                if i >= 4:
                    pe.wait_ge(gen_free, GEN * p + i - 3)
                if i >= 2:
                    hh, (c0, n) = (i - 2) // NC, CH[(i - 2) % NC]
                    for k in range(KQ):
                        w = slice(256 * k + P * hh, 256 * k + P * hh + P)
                        last = mm3(ps[:, i % 4, 0:n], wH[s][:, w], wL[s][:, w], cqH[:, k, c0:c0 + n],
                                   cqL[:, k, c0:c0 + n], k == 0, k == KQ - 1)
                else:
                    c0 = 512 * i
                    for k in range(KC):
                        w = slice(768 + P * k, 768 + P * k + P)
                        last = mm3(ps[:, i % 4, :], wH[s][:, w], wL[s][:, w], ckH[:, k, c0:c0 + 512],
                                   ckL[:, k, c0:c0 + 512], k == 0, k == KC - 1)
                last.then_inc(gen_ready, 1)

            def values(p):
                if p:
                    pe.wait_ge(t_free, tr_count(4 * p))
                else:
                    pe.wait_ge(n2_x, (KQ + KC) * NC)
                pe.wait_ge(split_lo, N_HEAD + 2 * p + 2)
                for j in range(2):
                    for x in range(4):
                        cols = slice(P * (4 * j + x), P * (4 * j + x) + P)
                        for k in range(KC):
                            last = mm3(ps[:, 4 + j, P * x:P * x + P], ckH[:, k, cols], ckL[:, k, cols],
                                       uvH[:, k, :], uvL[:, k, :], k == 0, k == KC - 1)
                    last.then_inc(vg_ready, 1)

            def score(u, qi):
                p, hh, blk = u // 4, u // 2 % 2, u % 2
                if u % 4 == 0 and qi < 2:
                    pe.wait_ge(gen_free, GEN * (p + 1) - 2 * (1 - qi))
                pe.wait_ge(q_lo, 2 * NC * p + NC * hh + (4 * blk + qi) // 3 + 1)
                if u == 0 and qi == 0:
                    pe.wait_ge(kr_lo, 2)
                    pe.wait_ge(made_r, 2)
                r, qt = 4 * u + qi, 4 * blk + qi
                if r >= 2:
                    pe.wait_ge(s_exp, r - 1)
                q = slice(P * qt, P * qt + P)
                for c0 in range(0, P * (qt + 1), 512):
                    n = min(512, P * (qt + 1) - c0)
                    out = ps[:, 2 * (r % 2) + c0 // 512, :]
                    last = mm3(out[:, 0:n], qH[0:QK, hh, q], qL[0:QK, hh, q], kH[0:QK, hh, c0:c0 + n],
                               kL[0:QK, hh, c0:c0 + n], True, c0 + n <= P * qt)
                last = nc.tensor.matmul(out[:, n - P:n], identR[:, :], cmaskR[:, :], start=False, stop=True)
                last.then_inc(s_ready, 1)

            def weigh(u):
                blk = u % 2
                nk = 4 * (blk + 1)

                def turn(kt):
                    x = tr_count(u) + kt
                    if x >= 2:
                        pe.wait_ge(t_free, x - 1)
                    for qi in range(max(0, kt - 4 * blk), 4):
                        if kt == 0 and qi < 3:
                            pe.wait_ge(s_pn, 3 * u + qi + 1)
                        elif kt == 0:
                            pe.wait_ge(s_pd, u + 1)
                        at = prob_at(4 * blk + qi) + P * kt
                        last = nc.tensor.transpose(ps[:, 4 + x % 2, P * qi:P * qi + P], prob[:, at:at + P],
                                                   ident[:, :])
                    last.then_inc(t_ready, 1)

                def product(kt):
                    x = tr_count(u) + kt
                    c0 = P * max(0, kt - 4 * blk)
                    pe.wait_ge(t_free, x + 1)
                    if kt == 0 and u >= 2:
                        pe.wait_ge(o_free, u - 1)
                    mm3(ps[:, 6 + u % 2, c0:512], hvH[:, kt, :], hvL[:, kt, :], pTH[:, x % 4, c0:512],
                        pTL[:, x % 4, c0:512], kt == 0, kt == nk - 1).then_inc(pv_x, 1)

                for kt in range(nk + 2):
                    for i in gens_at(u, kt):
                        query_key(u // 4 + 1, i)
                    qi = row_at(u, kt)
                    if qi is not None and not row_late(u, kt):
                        score(u + 1, qi)
                    if kt == 0:
                        pe.wait_ge(vg_free, 2 * (u // 4 + 1))
                    if kt < nk:
                        turn(kt)
                    if kt >= 2:
                        product(kt - 2)
                    if qi is not None and row_late(u, kt):
                        score(u + 1, qi)

            def sample_queries():
                pe.wait_ge(ld_uk, 16)
                pe.wait_ge(q_s, H)
                pe.wait_ge(s_exp, 4 * UNITS)
                for r in range(KC):
                    for h in range(H):
                        last = nc.tensor.matmul(ps[:, r, NS * h:NS * h + NS], ukT[:, h, P * r:P * r + P],
                                                qs[0:NOPE, :, h, :], start=True, stop=True)
                last.then_inc(q4_ready, 1)
                for r in range(KC):
                    last = nc.tensor.transpose(ps[0:NS, 2, P * r:P * r + P], ckv[:, r, SEQ:T], ident[:, :])
                last.then_inc(q4_ready, 1)

            def sample_scores(b):
                pe.wait_ge(cp_full[b % CB], 2 * 16 * PAGES * (b // CB + 1))
                if b == 0:
                    pe.wait_ge(q4_e, 3)
                elif b == 1:
                    pe.wait_ge(t_free, tr_count(UNITS))
                else:
                    pe.wait_ge(s4_exp, b - 1)
                    pe.wait_ge(t4_b, b - 1)
                q = slice(NS * b, NS * b + NS)
                for part in range(3):
                    bank = 3 * (b % 2) + part
                    if part == 1 and 3 <= b <= 4:
                        pe.wait_ge(n3_x, b - 2)
                    for r in range(3):
                        w = qlat[:, r, q] if r < 2 else qs[NOPE:QK, b, :, :].rearrange("p h t -> p (h t)")
                        if part < 2:
                            pg = slice(4 * part, 4 * part + 4)
                            x = cp[b % CB][:, pg, P * r:P * r + P] if r < 2 else cpr[NOPE:QK, b % CB, pg, :]
                            out = ps[0:NS, bank, :].rearrange("p (g n) -> p g n", g=4)
                        else:
                            x = ckv[:, r, SEQ:T] if r < 2 else kr[NOPE:QK, SEQ:T]
                            out = ps[0:NS, bank, 0:NS]
                        last = nc.tensor.matmul(out, w, x, start=r == 0, stop=r == 2)
                last.then_inc(s4_ready, 1)

            for i in range(GEN):
                query_key(0, i)
            values(0)
            for qi in range(4):
                score(0, qi)
            for u in range(UNITS):
                p = u // 4
                if u == UNITS - 1:
                    sample_queries()
                weigh(u)
                if u % 4 == 3 and u < UNITS - 1:
                    values(p + 1)

            sample_scores(0)
            for b in range(NB):
                pe.wait_ge(s4_n, b + 1)
                if b:
                    pe.wait_ge(t4_a, b)
                else:
                    pe.wait_ge(o_free, UNITS)
                for j in range(PAGES):
                    nc.tensor.transpose(ps[:, 6, NS * j:NS * j + NS], sp[:, b % 2, P * j:P * j + P],
                                        ident[0:NS, 0:NS])
                nc.tensor.transpose(ps[0:NS, 3 * (b % 2) + 2, NS:2 * NS], sp[:, b % 2, NEW:NEW + NS],
                                    ident[0:NS, 0:NS]).then_inc(t4_ready, 1)
                if b + 1 < NB:
                    sample_scores(b + 1)
                if 1 <= b <= 2:
                    sum_squares(J_N3 + b - 1, 3 * (b % 2) + 1, sqm, KG, CH[b - 1][1])
                pe.wait_ge(t4_a, b + 1)
                pe.wait_ge(t4_b, b + 1)
                if b:
                    pe.wait_ge(o4, b)
                for r in range(KC):
                    out = ps[:, 7, NS * r:NS * r + NS]
                    for j in range(PAGES):
                        nc.tensor.matmul(out, cp[b % CB][:, j, KVR + P * r:KVR + P * r + P], spT[:, j, :],
                                         start=j == 0, stop=False)
                    last = nc.tensor.matmul(out, ctok[:, P * r:P * r + P], spT[0:NS, PAGES, :],
                                            start=False, stop=True)
                last.then_inc(pv4, 1)
                if 1 <= b <= 2:
                    spread(J_N3 + b - 1, 3 * (b % 2) + 1, CH[b - 1][1])
            pe.wait_ge(o4, NB)
            pe.wait_ge(s4_exp, NB)
            pe.wait_ge(ld_uv, 16)
            for h in range(H):
                out = ps[VH * (h % 2):VH * (h % 2) + VH, 0, NS * (h // 2):NS * (h // 2) + NS]
                for r in range(KC):
                    last = nc.tensor.matmul(out, uvr[:, r, VH * h:VH * h + VH], olat[:, r, NS * h:NS * h + NS],
                                            start=r == 0, stop=r == KC - 1)
            last.then_inc(a4, 1)

            sum_squares(J_N3 + NC - 1, 6, sqm, KG, CH[NC - 1][1])

            def sum_x2(c):
                c0, n = CH[c]
                pe.wait_ge(n4_added, KD - 2)
                pe.wait_ge(nm_sq, J_N4 + c + 1)
                for i in range(2):
                    last = nc.tensor.matmul(ps[:, 4 + c, 0:n], ones[:, :], sq2[:, 2 * i, c0:c0 + n],
                                            start=i == 0, stop=i == 1)
                last.then_inc(nm_sum, 1)

            for m in range(KD):
                s = m % 2
                pe.wait_ge(split_lo, N_OUT + m + 1)
                for c, (c0, n) in enumerate(CH):
                    q = NC * m + c
                    if q >= 4:
                        pe.wait_ge(w_free, q - 3)
                    elif q == 0:
                        pe.wait_ge(a4_e, 1)
                    elif q == 1:
                        spread(J_N3 + NC - 1, 6, CH[NC - 1][1])
                    for j, k in enumerate(MIXED):
                        if m == 0:
                            pe.wait_ge(m_lo, 2 * KG * c + j + 1)
                        w = slice(P * k, P * k + P)
                        last = mm3(ps[:, q % 4, 0:n], wH[s][:, w], wL[s][:, w], mH[:, k, c0:c0 + n],
                                   mL[:, k, c0:c0 + n], j == 0, j == 2 * KG - 1)
                    last.then_inc(w_ready, 1)
                    if m == KD - 1 and c:
                        sum_x2(c - 1)
            spread(J_N4, 4, CH[0][1])
            sum_x2(NC - 1)

            def sum_y(c):
                n = CH[c][1]
                pe.wait_ge(n5_sq, KD * (c + 1))
                pe.wait_ge(n5_add, (KD - 2) * (c + 1))
                if c == 0:
                    pe.wait_ge(f_act, NC * NF)
                for m in (0, KD - 1):
                    last = nc.tensor.matmul(ps[:, c, 0:n], ones[:, :], sq3[:, square_at(c, m), 0:n],
                                            start=m == 0, stop=m == KD - 1)
                last.then_inc(nm_sum, 1)

            def feed_forward(first, i, last_turn=False):
                for s in range(2):
                    pe.wait_ge(split_lo, N_FF + 2 * s + (1 if first and s == 0 else 2) + BODY * i)
                    for c, (c0, n) in enumerate(CH):
                        q = NC * s + c
                        g0 = 2 * (q % 2)
                        if first and q < 2:
                            pe.wait_ge(w_free, NC * KD)
                        else:
                            pe.wait_ge(f_act, 2 * NC * i + (q - 1))
                        for hi, lo, b in ((wH, wL, g0), (upH, upL, g0 + 1)):
                            if first and s == 0 and b > g0:
                                if c + 1 < NC:
                                    spread(J_N4 + c + 1, 4 + c + 1, CH[c + 1][1])
                                pe.wait_ge(split_lo, N_FF + 2)
                            for k in range(KD):
                                if first and s == 0 and b == g0:
                                    pe.wait_ge(h2_lo, KD * c + k + 1)
                                w = slice(P * k, P * k + P)
                                last = mm3(ps[:, b, 0:n], hi[s][:, w], lo[s][:, w], h2H[:, k, c0:c0 + n],
                                           h2L[:, k, c0:c0 + n], k == 0, k == KD - 1)
                        last.then_inc(gu_ready, 1)
                pe.wait_ge(split_lo, N_FF + BODY + BODY * i)
                for c, (c0, n) in enumerate(CH):
                    pe.wait_ge(f_lo, 2 * NC * i + (NC + c + 1))
                    for m in range(KD):
                        r = KD * c + m
                        if first and r < 4:
                            pe.wait_ge(h2_x, KD * NC)
                        else:
                            pe.wait_ge(y_free, NC * KD * i + (r - 3))
                        w = slice(P * m, P * m + P)
                        for s in range(2):
                            last = mm3(ps[:, 4 + r % 4, 0:n], dnH[s][:, w], dnL[s][:, w], acH[:, s, c0:c0 + n],
                                       acL[:, s, c0:c0 + n], s == 0, s == 1)
                        last.then_inc(dn_ready, 1)
                        if last_turn and c and m == SUM_LAG - 1:
                            sum_y(c - 1)
                    if last_turn and c:
                        spread(J_N5 + c - 1, c - 1, CH[c - 1][1])

            feed_forward(True, 0)
            with pe.Fori(1, NF // 2 - 1) as i:
                feed_forward(False, i)
            feed_forward(False, NF // 2 - 1, last_turn=True)
            sum_y(NC - 1)
            spread(J_N5 + NC - 1, NC - 1, CH[NC - 1][1])

        @block.scalar
        def _(act):
            def hi(out, x, scale=1.0):
                return nc.scalar.activation(out, x, ACT.Copy, scale=scale)

            def squares(j, out, x):
                nc.scalar.activation(out, x, ACT.Square).then_inc(nm_sq, 1)

            def squares1(c):
                c0, n = CH1[c]
                act.wait_ge(ld_x[c], 16)
                if c:
                    act.wait_ge(nm_sum, J_N1 + c)
                squares(J_N1 + c, sq0[:, :, 0:n], x1[:, :, c0:c0 + n])

            def hi1(c):
                c0, n = CH1[c]
                for k in range(KD):
                    act.wait_ge(n1_x, KD * c + k + 1)
                    hi(hH[:, k, c0:c0 + n], x1[:, k, c0:c0 + n]).then_inc(n1_hi, 1)

            squares1(0)
            hi1(0)
            squares1(1)
            squares1(2)
            hi1(1)
            squares1(3)
            hi1(2)

            for t in range(NT + 1):
                if t == 2:
                    hi1(3)
                    act.wait_ge(ld_const, CONST)
                    hi(cmaskR[:, :], cmask[:, :]).then_inc(made_r, 1)
                    hi(identR[:, :], ident[:, :]).then_inc(made_r, 1)
                if t < NT:
                    m = rows(t)
                    act.wait_ge(v_ready, t + 1)
                    if t == 3:
                        act.wait_ge(nm_sum, J_N1 + len(CH1))
                    nc.scalar.activation(v_tile(t), ps[0:m, t % 4, :], ACT.Gelu).then_inc(v_gelu, 1)
                if t >= 2:
                    act.wait_ge(v_fin, t - 1)
                    hi(vH[:, t - 2, :], v_tile(t - 2)).then_inc(v_hi, 1)
            act.wait_ge(v_lo, NT - 1)
            for t in range(NT + 2):
                if t < NT:
                    m = rows(t)
                    act.wait_ge(u_ready, t + 1)
                    if t >= 2:
                        act.wait_ge(u_sq, t - 1)
                    nc.scalar.activation(ut[0:m, t % 2, :], ps[0:m, (t + 1) % 4, :], ACT.Gelu).then_inc(u_gelu, 1)
                if 1 <= t <= NT:
                    w = t - 1
                    m, s = rows(w), w % 4
                    act.wait_ge(u_g, w + 1)
                    nc.scalar.activation(ut[0:m, w % 2, :], mix[0:m, w, :], ACT.Square,
                                         accum_out=ssq[0:m, s:s + 1]).then_inc(u_sq, 1)
                if t >= 2:
                    w = t - 2
                    m = rows(w)
                    act.wait_ge(u_tr, w + 1)
                    hi(gT[:, :, P * w:P * w + m],
                       ps[:, 5 + w % 2, :].rearrange("p (k n) -> p k n", k=KG)[:, :, 0:m]).then_inc(u_out, 1)

            def move(q):
                c0, n = CH[q % NC]
                m = q // NC
                out = cq[:, m, c0:c0 + n] if m < KQ else ckv[:, m - KQ, c0:c0 + n]
                act.wait_ge(z_ready, q + 1)
                hi(out, ps[:, q % 4, 0:n]).then_inc(z_free, 1)

            def squares2(j):
                c0, n = CH[j % NC]
                k, x = (KQ, cq) if j < NC else (KC, ckv)
                act.wait_ge(z_free, NC * (KQ - 1) + j + 1 if j < NC else NC * (KQ + KC - 1) + j - NC + 1)
                if j >= 3:
                    act.wait_ge(nm_sum, J_N2 + j - 2)
                squares(J_N2 + j, sq1[:, j % 3, 0:k, 0:n], x[:, :, c0:c0 + n])

            def hi2(j):
                c0, n = CH[j % NC]
                act.wait_ge(n2_x, KQ * (j + 1) if j < NC else KQ * NC + KC * (j - NC + 1))
                out, x = (cqH, cq) if j < NC else (ckH, ckv)
                hi(out[:, :, c0:c0 + n], x[:, :, c0:c0 + n]).then_inc(n2_hi, 1)

            act.wait_ge(u_ready, NT)
            act.wait_ge(u_tr, NT)
            for q in range(9):
                move(q)
                if q >= 6:
                    squares2(q - 6)
            for q in range(9, 12):
                move(q)
            for q in range(12, 15):
                move(q)
                squares2(q - 12 + NC)
            for j in range(2 * NC):
                hi2(j)
            act.wait_ge(kr_ok, NC)
            for hh in range(2):
                hi(kH[NOPE:QK, hh, :], kr[NOPE:QK, 0:SEQ]).then_inc(kr_hi, 1)

            def move_gen(p, i):
                act.wait_ge(gen_ready, GEN * p + i + 1)
                if i == 0 and p:
                    act.wait_ge(s_ready, 16 * p)
                if i >= 2:
                    j = 2 * NC * p + i - 2
                    n = CH[(i - 2) % NC][1]
                    if j >= 3:
                        act.wait_ge(q_lo, j - 2)
                        act.wait_ge(q_s, (j - 2) // NC)
                    hi(qt_[0:NOPE, j % 3, 0:n], ps[0:NOPE, i % 4, 0:n]).then_inc(q_nope, 1)
                else:
                    c0 = 512 * i
                    for hh in range(2):
                        hi(kH[0:NOPE, hh, c0:c0 + 512],
                           ps[NOPE * hh:NOPE * hh + NOPE, i % 4, :]).then_inc(gen_hi, 1)
                if i >= 3:
                    query_hi(p, i - 1)

            def query_hi(p, i):
                j = 2 * NC * p + i - 2
                hh, (c0, n) = (i - 2) // NC, CH[(i - 2) % NC]
                act.wait_ge(q_rope, j + 1)
                n = min(n, SEQ - c0)
                hi(qH[0:QK, hh, c0:c0 + n], qt_[0:QK, j % 3, 0:n]).then_inc(q_hi, 1)
                if c0 + n == SEQ:
                    hi(qs[0:QK, :, 2 * p + hh, :],
                       qt_[0:QK, j % 3, n:n + NS].rearrange("p (b t) -> p b t", b=NB)).then_inc(q_s, 1)

            def move_values(p):
                for j in range(2):
                    act.wait_ge(vg_ready, 2 * p + j + 1)
                    hi(hvH[:, 4 * j:4 * j + 4, :].rearrange("p x n -> p (x n)"), ps[:, 4 + j, :]).then_inc(vg_hi, 1)

            def exponential(u, qi):
                r, qt = 4 * u + qi, 4 * (u % 2) + qi
                n, s = P * (qt + 1), r % 4
                act.wait_ge(s_nm, r + 1)
                if u >= 2 and qi == 0:
                    act.wait_ge(pv_x, tr_count(u - 1))
                nc.scalar.activation(prob[:, prob_at(qt):prob_at(qt) + n],
                                     psf[:, 1024 * (r % 2):1024 * (r % 2) + n], ACT.Exp,
                                     bias=nmx[:, s:s + 1], scale=SCALE,
                                     accum_out=sm[:, s:s + 1]).then_inc(s_exp, 1)

            def move_weighed(u):
                p, hh, blk = u // 4, u // 2 % 2, u % 2
                act.wait_ge(pv_x, tr_count(u + 1))
                part = slice(VH * hh, VH * hh + VH)
                hi(aT[part, p, 512 * blk:512 * blk + 512], ps[part, 6 + u % 2, :]).then_inc(o_free, 1)

            def move_turned(u):
                blk = u % 2
                for kt in range(4 * (blk + 1)):
                    x = tr_count(u) + kt
                    c0 = P * max(0, kt - 4 * blk)
                    act.wait_ge(t_ready, x + 1)
                    if x >= 4:
                        act.wait_ge(pv_x, x - 3)
                    hi(pTH[:, x % 4, c0:512], ps[:, 4 + x % 2, c0:512]).then_inc(t_hi, 1)
                    for i in gens_at(u, kt):
                        move_gen(u // 4 + 1, i)
                    if (qi := row_at(u, kt)) is not None:
                        if qi == 0 and u % 4 == 3:
                            query_hi(u // 4 + 1, GEN - 1)
                        exponential(u + 1, qi)
                    if kt == 1 and u:
                        move_weighed(u - 1)

            for i in range(GEN):
                move_gen(0, i)
            query_hi(0, GEN - 1)
            move_values(0)
            for qi in range(4):
                exponential(0, qi)
            def move_queries():
                act.wait_ge(q4_ready, 1)
                for r in range(KC):
                    hi(qlat[:, r, :].rearrange("p (b h t) -> p b h t", b=NB, h=H),
                       ps[:, r, :].rearrange("p (h b t) -> p b h t", b=NB, h=H)).then_inc(q4_e, 1)
                act.wait_ge(q4_ready, 2)
                hi(ctok[:, :], ps[0:NS, 2, 0:KVR]).then_inc(q4_e, 1)

            for u in range(UNITS):
                p = u // 4
                if u == UNITS - 1:
                    move_queries()
                move_turned(u)
                if u % 4 == 3 and u < UNITS - 1:
                    move_values(p + 1)
            move_weighed(UNITS - 1)

            def sample_exp(b):
                s = b % 2
                act.wait_ge(s4_nm, b + 1)
                if b >= 2:
                    act.wait_ge(t4_ready, b - 1)
                nc.scalar.activation(sp[:, s, :], psf[0:NS, 1536 * s:1536 * s + NEW + NS], ACT.Exp,
                                     bias=nmx[0:NS, s:s + 1], scale=SCALE,
                                     accum_out=sm[0:NS, s:s + 1]).then_inc(s4_exp, 1)

            def squares3(c):
                c0, n = CH[c]
                if c:
                    act.wait_ge(nm_sum, J_N3 + c)
                squares(J_N3 + c, sqm[:, :, 0:n], aT[:, :, c0:c0 + n])

            sample_exp(0)
            for b in range(NB):
                act.wait_ge(t4_ready, b + 1)
                if b:
                    act.wait_ge(pv4, b)
                hi(spT[:, 0:PAGES, :].rearrange("p j n -> p (j n)"), ps[:, 6, :]).then_inc(t4_a, 1)
                if b + 1 < NB:
                    sample_exp(b + 1)
                if b == 0:
                    act.wait_ge(o_free, UNITS)
                if b < 2:
                    squares3(b)
            act.wait_ge(a4, 1)
            hi(aT[:, :, SEQ:T], ps[:, 0, 0:KG * NS].rearrange("p (k n) -> p k n", k=KG)).then_inc(a4_e, 1)

            act.wait_ge(a4_e, 1)
            squares3(NC - 1)
            for c, (c0, n) in enumerate(CH):
                for k in MIXED:
                    x, gain = (aT, g_mla) if k < KG else (gT, g_gmlp)
                    if c == NC - 1 and k == 0:
                        act.wait_ge(n3_x, NC)
                    hi(mH[:, k, c0:c0 + n], x[:, k % KG, c0:c0 + n],
                       gain[:, k % KG:k % KG + 1]).then_inc(m_hi, 1)

            for m in range(KD - 1):
                act.wait_ge(w_free, NC * (m + 1))
                if m >= 3:
                    act.wait_ge(n4_added, m - 2)
                nc.scalar.activation(sq2[:, 1 + m % 2 if m else 0, :], x2[:, m, :], ACT.Square).then_inc(n4_sq, 1)
            act.wait_ge(n4_added, KD - 3)
            for c, (c0, n) in enumerate(CH):
                act.wait_ge(w_free, NC * (KD - 1) + c + 1)
                squares(J_N4 + c, sq2[:, 2, c0:c0 + n], x2[:, KD - 1, c0:c0 + n])

            def hi4(c):
                c0, n = CH[c]
                for k in range(KD):
                    j = KD * c + k
                    act.wait_ge(h2_x, j + 1)
                    hi(h2H[:, k, c0:c0 + n], htmp[:, j % 4, 0:n]).then_inc(h2_hi, 1)

            for c in range(NC - 1):
                hi4(c)

            def feed_forward(first, i):
                for q in range(2 * NC):
                    s, (c0, n) = q // NC, CH[q % NC]
                    act.wait_ge(gu_ready, 2 * NC * i + (q + 1))
                    if not (first and q < 2):
                        act.wait_ge(f_act, 2 * NC * i + (q - 1))
                    nc.scalar.activation(st[:, q % 2, 0:n], ps[:, 2 * (q % 2), 0:n], ACT.Silu).then_inc(f_silu, 1)
                    act.wait_ge(f_act, 2 * NC * i + (q + 1))
                    if not first:
                        act.wait_ge(dn_ready, NC * KD * i + (KD * (q % NC + 1) - NC * KD))
                    hi(acH[:, s, c0:c0 + n], av[:, q % 2, 0:n]).then_inc(f_hi, 1)
                    if first and q == 0:
                        hi4(NC - 1)

            feed_forward(True, 0)
            with act.Fori(1, NF // 2) as i:
                feed_forward(False, i)

            for c, (c0, n) in enumerate(CH):
                for m in range(KD):
                    r = KD * c + m
                    act.wait_ge(y_free, NC * KD * (NF // 2 - 1) + r + 1)
                    if c and 0 < m < KD - 1:
                        act.wait_ge(n5_add, (KD - 2) * (c - 1) + m)
                    elif c >= 2:
                        act.wait_ge(nm_sum, J_N5 + c - 1)
                    nc.scalar.activation(sq3[:, square_at(c, m), 0:n], x2[:, m, c0:c0 + n], ACT.Square).then_inc(n5_sq, 1)

        @block.vector
        def _(dve):
            def scaled(out, x, gain, factor):
                return nc.vector.scalar_tensor_tensor(out, x, gain, factor, ALU.mult, ALU.mult)

            def columns(j, bank, width, n, picked=diag):
                full, k = n // P, len(offsets(n))
                dve.wait_ge(nm_sum, j + 1)
                if j:
                    dve.wait_ge(nm_mean, j)
                    if picked is diag:
                        dve.wait_ge(nm_spread, j)
                last = nc.vector.tensor_tensor(picked[:, 0:full, :],
                                               ps[:, bank, 0:full * P].rearrange("p (i n) -> p i n", n=P),
                                               ident[:, :].unsqueeze(1).broadcast_to((P, full, P)), ALU.mult)
                if k > full:
                    last = nc.vector.tensor_tensor(picked[:, full, :], ps[:, bank, n - P:n], ident[:, :],
                                                   ALU.mult)
                last.then_inc(nm_pick, 1)
                dve.wait_ge(nm_pick, j + 1)
                nc.vector.tensor_reduce(sums[:, 0:k], picked[:, 0:k, :], AX.X, ALU.add).then_inc(nm_column, 1)
                dve.wait_ge(nm_column, j + 1)
                nc.vector.tensor_scalar(ms[:, j % 4, 0:k], sums[:, 0:k], 1.0 / width, EPS,
                                        ALU.mult, ALU.add).then_inc(nm_mean, 1)

            def diagonals(j, n):
                k = len(offsets(n))
                dve.wait_ge(nm_pow, j + 1)
                if j:
                    dve.wait_ge(nm_spread, j)
                nc.vector.tensor_tensor(diag[:, 0:k, :], ident[:, :].unsqueeze(1).broadcast_to((P, k, P)),
                                        rt[:, j % 4, 0:k].unsqueeze(2).broadcast_to((P, k, P)),
                                        ALU.mult).then_inc(nm_diag, 1)

            def factors(j, bank, width, n):
                columns(j, bank, width, n)
                diagonals(j, n)

            dve.wait_ge(ld_norm1, 32)
            dve.wait_ge(made, 3)

            def norm1(c):
                c0, n = CH1[c]
                factors(J_N1 + c, 4 + c, D, n)
                dve.wait_ge(nm_spread, J_N1 + c + 1)
                for k in range(KD + 1):
                    if k < KD:
                        x = x1[:, k, c0:c0 + n]
                        scaled(x, x, g1[:, k:k + 1], ps[:, 4 + c, 0:n]).then_inc(n1_x, 1)
                    if k:
                        dve.wait_ge(n1_hi, KD * c + k)
                        nc.vector.tensor_tensor(hL[:, k - 1, c0:c0 + n], x1[:, k - 1, c0:c0 + n],
                                                hH[:, k - 1, c0:c0 + n], ALU.subtract).then_inc(n1_lo, 1)

            def weights_lo(n, lo, hi):
                dve.wait_ge(split_hi, n + 1)
                nc.vector.tensor_tensor(lo, raw[:, n % 2, :], hi, ALU.subtract).then_inc(split_lo, 1)

            weights_lo(N_V, gw(vwL, 0), gw(vwH, 0))
            norm1(0)
            for j in range(1, 4):
                weights_lo(N_V + j, gw(vwL, j), gw(vwH, j))
            for c in range(1, 3):
                norm1(c)

            dve.wait_ge(ld_const, CONST)
            for t in range(NT + 1):
                if t == 2:
                    norm1(3)
                if t < NT:
                    m, s = rows(t), t % 2
                    dve.wait_ge(v_gelu, t + 1)
                    nc.vector.bn_stats(stat6[0:m, s, :], v_tile(t)).then_inc(v_b1, 1)
                    dve.wait_ge(v_b1, t + 1)
                    nc.vector.bn_aggr(mv[0:m, s, :], stat6[0:m, s, :]).then_inc(v_b2, 1)
                    dve.wait_ge(v_b2, t + 1)
                    nc.vector.tensor_scalar(ve[0:m, t % 4:t % 4 + 1], mv[0:m, s, 1:2], EPS, None,
                                            ALU.add).then_inc(v_ve, 1)
                if t >= 1:
                    w = t - 1
                    m, x = rows(w), v_tile(w)
                    dve.wait_ge(v_rv, w + 1)
                    nc.vector.tensor_scalar(x, x, mv[0:m, w % 2, 0:1], rv[0:m, w % 4:w % 4 + 1], ALU.subtract,
                                            ALU.mult).then_inc(v_n1, 1)
                    dve.wait_ge(v_n1, w + 1)
                    nc.vector.tensor_tensor(x, x, vgb[0:m, 0, :], ALU.mult).then_inc(v_n2, 1)
                    dve.wait_ge(v_n2, w + 1)
                    nc.vector.tensor_tensor(x, x, vgb[0:m, 1, :], ALU.add).then_inc(v_fin, 1)
                if t in U_LOWS:
                    j = U_LOWS.index(t)
                    weights_lo(N_U + j, gw(uwL, j), gw(uwH, j))
            for g in range(G):
                dve.wait_ge(sp_ready, g + 1)
                nc.vector.tensor_scalar(mix[:, 0:8, GD * g:GD * g + GD],
                                        ps[:, 4 + g % 4, :].rearrange("p (c n) -> p c n", c=8),
                                        bs[:, g:g + 1], None, ALU.add).then_inc(sp_free, 1)
            dve.wait_ge(sp_ready, G + 1)
            grp = "p (g n) -> p g n"
            nc.vector.tensor_tensor(mix[0:NS, 8, :].rearrange(grp, g=G), ps[0:NS, 4, :].rearrange(grp, g=G),
                                    bs8[:, :].unsqueeze(2).broadcast_to((NS, G, GD)), ALU.add).then_inc(sp_free, 1)
            dve.wait_ge(sp_free, G + 1)
            for t in range(NT + 1):
                if t < NT:
                    m = rows(t)
                    dve.wait_ge(u_gelu, t + 1)
                    nc.vector.tensor_tensor(mix[0:m, t, :], ut[0:m, t % 2, :], mix[0:m, t, :],
                                            ALU.mult).then_inc(u_g, 1)
                if t >= 1:
                    w = t - 1
                    m, s = rows(w), slice(w % 4, w % 4 + 1)
                    dve.wait_ge(u_sq, w + 1)
                    nc.vector.tensor_scalar(ve[0:m, s], ssq[0:m, s], 1.0 / GW, EPS, ALU.mult,
                                            ALU.add).then_inc(u_ve, 1)
                    dve.wait_ge(u_rv, w + 1)
                    nc.vector.tensor_scalar(mix[0:m, w, :], mix[0:m, w, :], rv[0:m, s], None,
                                            ALU.mult).then_inc(u_gn, 1)

            def norm2(j):
                c0, n = CH[j % NC]
                k_, x_, g_, out = (KQ, cq, gq, (cqH, cqL)) if j < NC else (KC, ckv, gkv, (ckH, ckL))
                factors(J_N2 + j, 4 + j % NC, QR if j < NC else KVR, n)
                if j == 2 * NC - 1:
                    for c in range(NC, j):
                        low2(c)
                dve.wait_ge(nm_spread, J_N2 + j + 1)
                for k in range(k_):
                    x = x_[:, k, c0:c0 + n]
                    scaled(x, x, g_[:, k:k + 1], ps[:, 4 + j % NC, 0:n]).then_inc(n2_x, 1)

            def low2(j):
                c0, n = CH[j % NC]
                x, h, lo = (cq, cqH, cqL) if j < NC else (ckv, ckH, ckL)
                dve.wait_ge(n2_hi, j + 1)
                nc.vector.tensor_tensor(lo[:, :, c0:c0 + n], x[:, :, c0:c0 + n], h[:, :, c0:c0 + n],
                                        ALU.subtract).then_inc(n2_lo, 1)

            for j in range(NC):
                norm2(j)
            for j in range(NC):
                low2(j)
            def rope_key(c):
                c0, n = CH[c]
                b = (NC * (KQ + KC) + c) % 4
                cols = slice(c0, c0 + n)
                nc.vector.tensor_tensor(kr[NOPE:QK, cols], ps[NOPE:QK, b, 0:n], cs[NOPE:QK, cols],
                                        ALU.mult).then_inc(kr_a, 1)
                if c:
                    dve.wait_ge(kr_ok, c)
                nc.vector.tensor_tensor(qr2[NOPE:QK, 0:n], ps[QK:P, b, 0:n], cs[QK:P, cols],
                                        ALU.mult).then_inc(kr_a, 1)
                dve.wait_ge(kr_a, 2 * c + 2)
                nc.vector.tensor_tensor(kr[NOPE:QK, cols], kr[NOPE:QK, cols], qr2[NOPE:QK, 0:n],
                                        ALU.add).then_inc(kr_ok, 1)

            for j in range(NC, 2 * NC):
                norm2(j)
            dve.wait_ge(ld_cs, 16)
            dve.wait_ge(z_ready, NC * (KQ + KC + 1))
            rope_key(0)
            rope_key(1)
            low2(2 * NC - 1)
            rope_key(2)
            dve.wait_ge(kr_hi, 1)
            nc.vector.tensor_tensor(kL[NOPE:QK, 0, :], kr[NOPE:QK, 0:SEQ], kH[NOPE:QK, 0, :],
                                    ALU.subtract).then_inc(kr_lo, 1)

            def move_gen(p, i):
                dve.wait_ge(gen_ready, GEN * p + i + 1)
                if i >= 2:
                    j = 2 * NC * p + i - 2
                    c0, n = CH[(i - 2) % NC]
                    cols = slice(c0, c0 + n)
                    x = qt_[NOPE:QK, j % 3, 0:n]
                    if j >= 3:
                        dve.wait_ge(q_lo, j - 2)
                        dve.wait_ge(q_s, (j - 2) // NC)
                    nc.vector.tensor_tensor(x, ps[NOPE:QK, i % 4, 0:n], cs[NOPE:QK, cols],
                                            ALU.mult).then_inc(q_cos, 1)
                    dve.wait_ge(q_nope, j + 1)
                    if j:
                        dve.wait_ge(q_rope, j)
                    else:
                        dve.wait_ge(kr_ok, NC)
                    nc.vector.tensor_tensor(qr2[NOPE:QK, 0:n], ps[QK:P, i % 4, 0:n], cs[QK:P, cols],
                                            ALU.mult).then_inc(gen_free, 1)
                    dve.wait_ge(gen_free, GEN * p + i + 1)
                    dve.wait_ge(q_cos, j + 1)
                    nc.vector.tensor_tensor(x, x, qr2[NOPE:QK, 0:n], ALU.add).then_inc(q_rope, 1)
                else:
                    c0 = 512 * i
                    for hh in range(2):
                        dve.wait_ge(gen_hi, 4 * p + 2 * i + hh + 1)
                        ins = nc.vector.tensor_tensor(kL[0:NOPE, hh, c0:c0 + 512],
                                                      ps[NOPE * hh:NOPE * hh + NOPE, i % 4, :],
                                                      kH[0:NOPE, hh, c0:c0 + 512], ALU.subtract)
                    ins.then_inc(gen_free, 1)

            def move_values(p):
                flat = "p x n -> p (x n)"
                for j in range(2):
                    dve.wait_ge(vg_hi, 2 * p + j + 1)
                    nc.vector.tensor_tensor(hvL[:, 4 * j:4 * j + 4, :].rearrange(flat), ps[:, 4 + j, :],
                                            hvH[:, 4 * j:4 * j + 4, :].rearrange(flat),
                                            ALU.subtract).then_inc(vg_free, 1)

            def invert(r):
                s = slice(r % 4, r % 4 + 1)
                dve.wait_ge(s_exp, r + 1)
                u, qi = r // 4, r % 4
                if u and qi < 3:
                    dve.wait_ge(s_pn, 3 * (u - 1) + qi + 1)
                elif u:
                    dve.wait_ge(s_pd, u)
                nc.vector.reciprocal(rsm[:, s], sm[:, s]).then_inc(s_rc, 1)
                if qi == 3:
                    qt = 4 * (u % 2) + 3
                    row = prob[:, prob_at(qt):prob_at(qt + 1)]
                    dve.wait_ge(s_rc, r + 1)
                    nc.vector.tensor_scalar(row, row, rsm[:, s], None, ALU.mult).then_inc(s_pd, 1)

            def maximum(u, qi):
                r, qt = 4 * u + qi, 4 * (u % 2) + qi
                at, s = 1024 * (r % 2), slice(r % 4, r % 4 + 1)
                dve.wait_ge(s_ready, r + 1)
                nc.vector.tensor_reduce(mx[:, s], psf[:, at:at + P * (qt + 1)], AX.X,
                                        ALU.max).then_inc(s_mx, 1)
                dve.wait_ge(s_mx, r + 1)
                nc.vector.tensor_scalar(nmx[:, s], mx[:, s], -SCALE, None, ALU.mult).then_inc(s_nm, 1)

            def move_turned(u):
                blk = u % 2
                for kt in range(4 * (blk + 1)):
                    x = tr_count(u) + kt
                    c0 = P * max(0, kt - 4 * blk)
                    qi = row_at(u, kt)
                    if qi is not None and kt < 4 * blk + 3 and not row_late(u, kt):
                        maximum(u + 1, qi)
                    if qi:
                        invert(4 * (u + 1) + qi - 1)
                    dve.wait_ge(t_hi, x + 1)
                    nc.vector.tensor_tensor(pTL[:, x % 4, c0:512], ps[:, 4 + x % 2, c0:512],
                                            pTH[:, x % 4, c0:512], ALU.subtract).then_inc(t_free, 1)
                    for i in gens_at(u, kt):
                        move_gen(u // 4 + 1, i)
                    if qi is not None and (kt == 4 * blk + 3 or row_late(u, kt)):
                        maximum(u + 1, qi)
                    if qi == 3:
                        invert(4 * (u + 1) + qi)

            for i in range(GEN):
                move_gen(0, i)
            move_values(0)
            for qi in range(4):
                maximum(0, qi)
                if qi:
                    invert(qi - 1)
            invert(3)
            for u in range(UNITS):
                p = u // 4
                move_turned(u)
                if u % 4 == 3 and u < UNITS - 1:
                    move_values(p + 1)

            def sample_max(b):
                s = b % 2
                new = psf[0:NS, 1536 * s + NEW:1536 * s + NEW + NS]
                dve.wait_ge(s4_ready, b + 1)
                nc.vector.tensor_tensor(new, new, smask[:, b, :], ALU.add).then_inc(s4_mk, 1)
                dve.wait_ge(s4_mk, b + 1)
                nc.vector.tensor_reduce(mx[0:NS, s:s + 1], psf[0:NS, 1536 * s:1536 * s + NEW + NS], AX.X,
                                        ALU.max).then_inc(s4_mx, 1)
                dve.wait_ge(s4_mx, b + 1)
                nc.vector.tensor_scalar(nmx[0:NS, s:s + 1], mx[0:NS, s:s + 1], -SCALE, None,
                                        ALU.mult).then_inc(s4_nm, 1)

            def sample_norm(b):
                s = b % 2
                dve.wait_ge(s4_exp, b + 1)
                nc.vector.reciprocal(rsm[0:NS, s:s + 1], sm[0:NS, s:s + 1]).then_inc(s4_rc, 1)
                dve.wait_ge(s4_rc, b + 1)
                nc.vector.tensor_scalar(sp[:, s, :], sp[:, s, :], rsm[0:NS, s:s + 1], None,
                                        ALU.mult).then_inc(s4_n, 1)

            dve.wait_ge(s_pn, 3 * UNITS)
            dve.wait_ge(s_pd, UNITS)
            def scale_heads(c, bank):
                c0, n = CH[c]
                dve.wait_ge(nm_spread, J_N3 + c + 1)
                x = aT[:, :, c0:c0 + n]
                nc.vector.tensor_tensor(x, x, ps[:, bank, 0:n].unsqueeze(1).broadcast_to((P, KG, n)),
                                        ALU.mult).then_inc(n3_x, 1)

            sample_max(0)
            sample_norm(0)
            for b in range(NB):
                dve.wait_ge(t4_ready, b + 1)
                if b:
                    dve.wait_ge(pv4, b)
                nc.vector.tensor_copy(spT[0:NS, PAGES, :],
                                      ps[0:NS, 3 * (b % 2) + 2, NS:2 * NS]).then_inc(t4_b, 1)
                if b + 1 < NB:
                    sample_max(b + 1)
                    sample_norm(b + 1)
                if 1 <= b <= 2:
                    factors(J_N3 + b - 1, 3 * (b % 2) + 1, GW, CH[b - 1][1])
                dve.wait_ge(pv4, b + 1)
                out = olat[:, :, :].rearrange("p r (h n) -> p r h n", h=H)[:, :, :, TS * b:TS * b + TS]
                nc.vector.tensor_copy(out, ps[:, 7, 0:KC * NS].rearrange("p (r h t) -> p r h t", r=KC,
                                                                       h=H)).then_inc(o4, 1)
                if 1 <= b <= 2:
                    scale_heads(b - 1, 3 * (b % 2) + 1)

            dve.wait_ge(a4, 1)
            for c, (c0, n) in enumerate(CH):
                for j, k in enumerate(MIXED):
                    x, gain = (aT, g_mla) if k < KG else (gT, g_gmlp)
                    if c == 0 and k == 0:
                        factors(J_N3 + NC - 1, 6, GW, CH[NC - 1][1])
                    if c == NC - 1 and k == 0:
                        scale_heads(NC - 1, 6)
                    dve.wait_ge(m_hi, 2 * KG * c + j + 1)
                    nc.vector.scalar_tensor_tensor(mL[:, k, c0:c0 + n], x[:, k % KG, c0:c0 + n],
                                                   gain[:, k % KG:k % KG + 1], mH[:, k, c0:c0 + n],
                                                   ALU.mult, ALU.subtract).then_inc(m_lo, 1)

            def columns4(c):
                columns(J_N4 + c, 4 + c, D, CH[c][1], picked)

            for m in range(KD):
                dve.wait_ge(ld_x2[m // 2], 16)
                for c, (c0, n) in enumerate(CH):
                    q = NC * m + c
                    x = x2[:, m, c0:c0 + n]
                    dve.wait_ge(w_ready, q + 1)
                    nc.vector.tensor_tensor(x, x, ps[:, q % 4, 0:n], ALU.add).then_inc(w_free, 1)
                    if q == NC * KD - 2:
                        columns4(0)
                        diagonals(J_N4, CH[0][1])


            def norm4(c):
                c0, n = CH[c]
                dve.wait_ge(nm_spread, J_N4 + c + 1)
                dve.wait_ge(w_free, NC * KD)
                for k in range(KD + 1):
                    j = KD * c + k
                    if k < KD:
                        if j >= 4:
                            dve.wait_ge(h2_lo, j - 3)
                        scaled(htmp[:, j % 4, 0:n], x2[:, k, c0:c0 + n], g2[:, k:k + 1],
                               ps[:, 4 + c, 0:n]).then_inc(h2_x, 1)
                    if c == 0 and k:
                        dve.wait_ge(h2_hi, k)
                        nc.vector.tensor_tensor(h2L[:, k - 1, 0:n], htmp[:, (k - 1) % 4, 0:n],
                                                h2H[:, k - 1, 0:n], ALU.subtract).then_inc(h2_lo, 1)
                if c + 1 < NC:
                    diagonals(J_N4 + c + 1, CH[c + 1][1])
                if c == 0:
                    columns4(2)

            columns4(1)
            for c in range(NC - 1):
                norm4(c)

            def scale_y(c, k):
                c0, n = CH[c]
                if k == 0:
                    dve.wait_ge(nm_spread, J_N5 + c + 1)
                x = x2[:, k, c0:c0 + n]
                scaled(x, x, gf[:, k:k + 1], ps[:, c, 0:n]).then_inc(n5_x, 1)

            def feed_forward(first, i, last_turn=False):
                for q in range(2 * NC):
                    s, (c0, n) = q // NC, CH[q % NC]
                    a = av[:, q % 2, 0:n]
                    dve.wait_ge(f_silu, 2 * NC * i + (q + 1))
                    if not (first and q < 2):
                        dve.wait_ge(f_lo, 2 * NC * i + (q - 1))
                    nc.vector.tensor_tensor(a, st[:, q % 2, 0:n], ps[:, 2 * (q % 2) + 1, 0:n],
                                            ALU.mult).then_inc(f_act, 1)
                    dve.wait_ge(f_hi, 2 * NC * i + (q + 1))
                    nc.vector.tensor_tensor(acL[:, s, c0:c0 + n], a, acH[:, s, c0:c0 + n],
                                            ALU.subtract).then_inc(f_lo, 1)
                    if first and q == 0:
                        norm4(NC - 1)
                for c, (c0, n) in enumerate(CH):
                    for m in range(KD):
                        r = KD * c + m
                        x = x2[:, m, c0:c0 + n]
                        dve.wait_ge(dn_ready, NC * KD * i + (r + 1))
                        nc.vector.tensor_tensor(x, x, ps[:, 4 + r % 4, 0:n], ALU.add).then_inc(y_free, 1)
                        if last_turn:
                            if c and m == SUM_LAG:
                                factors(J_N5 + c - 1, c - 1, D, CH[c - 1][1])
                            if c == NC - 1:
                                scale_y(0, m)

            feed_forward(True, 0)
            with dve.Fori(1, NF // 2 - 1) as i:
                feed_forward(False, i)
            feed_forward(False, NF // 2 - 1, last_turn=True)
            dve.wait_ge(y_free, NC * KD * (NF // 2))
            for k in range(KD // 2):
                scale_y(1, k)
            factors(J_N5 + 2, 2, D, CH[2][1])
            for k in range(KD // 2, KD):
                scale_y(1, k)
            for k in range(KD):
                scale_y(2, k)


def _by_tile(v, k):
    return v.reshape(k, P).T


def _pieces(w, k, step=P):
    m = w.shape[1] // step
    return w.reshape(k, P, m, step).transpose(2, 1, 0, 3).reshape(m, P, k * step)


def kernel(**inputs):
    import numpy as np
    import concourse.bacc as bacc
    from concourse.bass_utils import run_bass_kernel_spmd

    a = {k: np.asarray(v) for k, v in inputs.items()}
    f = np.float32
    x = np.concatenate([a["x_prompt"].reshape(SEQ, D), a["x_sample"].reshape(NS, D)])
    arr = {"x": x.T.reshape(KD, P, T).transpose(1, 0, 2)}
    w_in = a["w_in"][0]
    o_kr = QR + KVR
    o_u = o_kr + ROPE
    o_v = o_u + GW
    half = ROPE // 2
    arr["w_v"] = w_in[:, o_v:].reshape(4, 2, P, GW).transpose(0, 2, 1, 3).reshape(4, P, 1024)
    arr["w_u"] = w_in[:, o_u:o_v].reshape(4, 2, P, GW).transpose(0, 2, 1, 3).reshape(4, P, 1024)
    k_rope = w_in[:, o_kr:o_u]
    k_tile = np.concatenate([np.zeros((D, NOPE), f), k_rope, k_rope[:, half:], k_rope[:, :half]], 1)
    arr["w_in"] = _pieces(np.concatenate([w_in[:, :o_kr], k_tile], 1), KD)
    arr["w_sp"] = a["w_spatial"][0].transpose(2, 0, 1).reshape(P, G * P)
    wbd = np.zeros((NB, TS, G, NB, TS), f)
    for b in range(NB):
        wbd[b, :, :, b, :] = a["w_spatial"][0][:, :TS, :TS].transpose(2, 0, 1)
    arr["wbd"] = wbd.reshape(NS, G, NS)
    arr["bs"] = a["b_spatial"][0].T
    arr["bs8"] = np.tile(a["b_spatial"][0][:, :TS].T, (NB, 1))
    arr["vgb"] = np.broadcast_to(np.stack([a["v_norm_g"][0], a["v_norm_b"][0]]), (P, 2, GW))
    wq = a["w_q_up"][0].reshape(QR, H, QK)
    wq = np.concatenate([wq, wq[:, :, NOPE + half:], wq[:, :, NOPE:NOPE + half]], 2)
    wq = _pieces(wq.reshape(QR, H * P), KQ, 2 * P)
    wk = _pieces(a["w_uk"][0].reshape(KVR, H * NOPE), KC)
    arr["w_qk"] = np.concatenate([wq, wk], 2)
    arr["w_uv"] = _pieces(a["w_uv"][0].reshape(KVR, H * VH), KC)
    arr["w_ukT"] = a["w_uk"][0].transpose(2, 1, 0)
    arr["w_uvr"] = a["w_uv"][0].reshape(KC, P, GW).transpose(1, 0, 2)
    pool = a["cache_ckv"].shape[1]
    rec = np.zeros((pool, P, REC), f)
    ckv = a["cache_ckv"][0]
    rec[:, :, 0:KVR] = ckv.transpose(0, 2, 1).reshape(pool, KC, P, PAGE).transpose(0, 2, 1, 3).reshape(pool, P, KVR)
    rec[:, :, KVR:2 * KVR] = ckv
    arr["cache"] = rec
    arr["cache_r"] = a["cache_krope"][0].transpose(0, 2, 1)
    arr["pages"] = a["page_table"].reshape(1, NB * PAGES)
    arr["w_out"] = _pieces(a["w_out"][0], 2 * KG)
    gate, up = _pieces(a["w_gate"][0], KD), _pieces(a["w_up"][0], KD)
    down = a["w_down"][0].reshape(NF, P, D)
    arr["w_ff"] = np.stack([gate[0::2], up[0::2], gate[1::2], up[1::2], down[0::2], down[1::2]],
                           1).reshape(3 * NF, P, 1024)
    for name, key, k in (("g1", "norm1_g", KD), ("gq", "q_norm_g", KQ), ("gkv", "kv_norm_g", KC),
                         ("g_mla", "out_norm_mla_g", KG), ("g_gmlp", "out_norm_gmlp_g", KG),
                         ("g2", "norm2_g", KD)):
        arr[name] = _by_tile(a[key][0], k)
    arr["gf"] = _by_tile(a["final_norm_g"], KD)
    pos = np.concatenate([np.arange(SEQ), np.tile(NEW + np.arange(TS), NB)]).astype(f)
    inv = (10000.0 ** (-np.arange(half, dtype=f) / half)).astype(f)
    ang = (pos[None, :] * inv[:, None]).astype(f)
    cs = np.zeros((P, T), f)
    cs[NOPE:QK] = np.tile(np.cos(ang), (2, 1))
    cs[QK:P] = np.concatenate([-np.sin(ang), np.sin(ang)])
    arr["cs"] = cs
    arr["ident"] = np.eye(P, dtype=f)
    arr["cmask"] = np.where(np.arange(P)[None, :] <= np.arange(P)[:, None], 0, -1e30).astype(f)
    b_, t_ = np.arange(NS) // TS, np.arange(NS) % TS
    qtok = np.arange(NS) % TS
    see = (b_[None, None, :] == np.arange(NB)[None, :, None]) & (t_[None, None, :] <= qtok[:, None, None])
    arr["smask"] = np.where(see, 0, -1e30).astype(f)

    nc = bacc.Bacc("TRN2", target_bir_lowering=False, num_devices=1)
    dram, sent = {}, {}
    for name, v in arr.items():
        v = np.ascontiguousarray(v)
        sent["in_" + name] = v
        dram[name] = nc.dram_tensor("in_" + name, v.shape, mybir.dt.from_np(v.dtype), kind="ExternalInput").ap()
    for name, shape in (("y", (P, KD, T)), ("ckv_out", (P, KC, T)), ("kr_out", (ROPE, T)), ("v_out", (NS, GW))):
        dram[name] = nc.dram_tensor("out_" + name, shape, F32, kind="ExternalOutput").ap()
    build(nc, dram)
    got = run_bass_kernel_spmd(nc, [sent], core_ids=[0]).results[0]
    y = got["out_y"].transpose(1, 0, 2).reshape(D, T).T
    c = got["out_ckv_out"].transpose(1, 0, 2).reshape(KVR, T).T
    k = got["out_kr_out"].T
    return (y[:SEQ].reshape(1, SEQ, D), y[SEQ:].reshape(NB, TS, D),
            c[:SEQ].reshape(1, 1, SEQ, KVR), k[:SEQ].reshape(1, 1, SEQ, ROPE),
            c[SEQ:].reshape(1, NB, TS, KVR), k[SEQ:].reshape(1, NB, TS, ROPE),
            got["out_v_out"].reshape(1, NB, TS, GW))
```
